# Optimizing a Trainium2 kernel written in Bass

```python
import jax
import jax.numpy as jnp
from jax import lax
import numpy as np

D_MODEL = 1024
BATCH = 1
SEQ = 512
DEPTH = 1

CTX_LEN = 256
GRID_W = 64
N_SUBLAYERS = 3
D_FF = 2816
FFN_HALF = 0.5
GLA_HEADS = 4
GLA_DK = 64
GLA_DV = 128
GLA_GATE_RANK = 16
GLA_GATE_NORMALIZER = 16.0
HGRN_HEADS = 4
HGRN_DK = 128
HGRN_DV = 128
GLA_QK = GLA_HEADS * GLA_DK
GLA_V = GLA_HEADS * GLA_DV
HGRN_K = HGRN_HEADS * HGRN_DK
HGRN_V = HGRN_HEADS * HGRN_DV
MIX_WIDTH = GLA_V + HGRN_V
IN_SPLITS = (GLA_QK, GLA_QK, GLA_V, GLA_V, GLA_GATE_RANK, GLA_GATE_RANK, HGRN_K, HGRN_K, HGRN_K, HGRN_V, HGRN_V)
IN_WIDTH = sum(IN_SPLITS)
CHUNK = 32
LN_EPS = 1e-5
NORM_EPS = 1e-6
POS_THETA = 10000.0
DN_ALPHA = (2.0 * DEPTH) ** 0.25
DN_BETA = (8.0 * DEPTH) ** -0.25

kernel_name = "hybrid_gla_hgrn2_dit_layer"

def layer_norm(x, gain=None, bias=None):
    xf = x.astype(jnp.float32)
    mu = jnp.mean(xf, axis=-1, keepdims=True)
    var = jnp.mean(jnp.square(xf - mu), axis=-1, keepdims=True)
    y = (xf - mu) * lax.rsqrt(var + LN_EPS)
    if gain is not None:
        y = y * gain.astype(jnp.float32) + bias.astype(jnp.float32)
    return y.astype(x.dtype)

def modulate(x, m, i):
    return layer_norm(x) * (1.0 + m[:, 3 * i][:, None, :]) + m[:, 3 * i + 1][:, None, :]

def residual_post_norm(x, y, gate, weight, gain, bias):
    return layer_norm(DN_ALPHA * x + weight * gate[:, None, :] * y, gain, bias)

def swiglu(h, w_in, w_out):
    gate, up = jnp.split(h @ w_in, 2, axis=-1)
    return (jax.nn.silu(gate) * up) @ w_out

def sincos_2d(rows, width, dim):
    r = jnp.repeat(jnp.arange(rows), width)
    col = jnp.tile(jnp.arange(width), rows)
    quarter = dim // 4
    omega = 1.0 / POS_THETA ** (jnp.arange(quarter, dtype=jnp.float32) / quarter)

    def emb(p):
        a = p.astype(jnp.float32)[:, None] * omega[None, :]
        return jnp.concatenate([jnp.sin(a), jnp.cos(a)], axis=-1)

    return jnp.concatenate([emb(r), emb(col)], axis=-1)

def to_heads(a, n_heads):
    b, t, _ = a.shape
    return a.reshape(b, t, n_heads, -1).transpose(0, 2, 1, 3)

def from_heads(a):
    b, h, t, d = a.shape
    return a.transpose(0, 2, 1, 3).reshape(b, t, h * d)

def chunk_gated_linear_attention(q, k, v, log_f, s0):
    bsz, nh, t, _ = q.shape
    dv = v.shape[-1]
    n_chunks = t // CHUNK

    def split(a):
        return a.astype(jnp.float32).reshape(bsz, nh, n_chunks, CHUNK, a.shape[-1]).transpose(2, 0, 1, 3, 4)

    lower_tri = jnp.tril(jnp.ones((CHUNK, CHUNK), dtype=bool))

    def step(s, blk):
        qb, kb, vb, gb = blk
        b = jnp.cumsum(gb, axis=-2)
        b_last = b[..., -1:, :]
        q_dec = qb * jnp.exp(b)
        k_inv = kb * jnp.exp(-b)
        k_tail = kb * jnp.exp(b_last - b)
        att = jnp.where(lower_tri, jnp.einsum("bhik,bhjk->bhij", q_dec, k_inv), 0.0)
        o = jnp.einsum("bhij,bhjv->bhiv", att, vb) + jnp.einsum("bhik,bhkv->bhiv", q_dec, s)
        s_new = jnp.swapaxes(jnp.exp(b_last), -1, -2) * s + jnp.einsum("bhjk,bhjv->bhkv", k_tail, vb)
        return s_new, o

    s_final, o = lax.scan(step, s0.astype(jnp.float32), (split(q), split(k), split(v), split(log_f)))
    return o.transpose(1, 2, 0, 3, 4).reshape(bsz, nh, t, dv), s_final

def bidirectional_scan(lat, ctx):
    q, k_f, k_b, v, g_f, g_b = lat
    qc, kc_f, kc_b, vc, gc_f, gc_b = ctx

    def flip(a):
        return jnp.flip(a, axis=2)

    zero = jnp.zeros(qc.shape[:2] + (qc.shape[-1], vc.shape[-1]), jnp.float32)
    oc_f, sc_f = chunk_gated_linear_attention(qc, kc_f, vc, gc_f, zero)
    oc_b, sc_b = chunk_gated_linear_attention(flip(qc), flip(kc_b), flip(vc), flip(gc_b), zero)
    o_f, _ = chunk_gated_linear_attention(q, k_f, v, g_f, sc_f)
    o_b, _ = chunk_gated_linear_attention(flip(q), flip(k_b), flip(v), flip(g_b), sc_b)
    return o_f + flip(o_b), oc_f + flip(oc_b)

def mixer_features(h, w_in, a2_f, a2_b, a_bias_f, a_bias_b, lb_f, lb_b):
    split_points = np.cumsum(IN_SPLITS)[:-1].tolist()
    (g_q, g_k, g_v, g_gate, g_lr_f, g_lr_b, r_q, r_f_f, r_f_b, r_i, r_gate) = jnp.split(h @ w_in, split_points, axis=-1)

    def gla_log_decay(lr, a2, bias):
        return to_heads(jax.nn.log_sigmoid((lr @ a2 + bias).astype(jnp.float32)) / GLA_GATE_NORMALIZER, GLA_HEADS)

    def hgrn_forget(z, lb):
        f = lb + (1.0 - lb) * jax.nn.sigmoid(z.astype(jnp.float32))
        return to_heads(jnp.log(f), HGRN_HEADS), to_heads(1.0 - f, HGRN_HEADS)

    k_gla = to_heads(g_k, GLA_HEADS)
    gla = (to_heads(g_q * GLA_DK ** -0.5, GLA_HEADS), k_gla, k_gla, to_heads(g_v, GLA_HEADS),
           gla_log_decay(g_lr_f, a2_f, a_bias_f), gla_log_decay(g_lr_b, a2_b, a_bias_b))
    logf_f, k_f = hgrn_forget(r_f_f, lb_f)
    logf_b, k_b = hgrn_forget(r_f_b, lb_b)
    hgrn = (to_heads(jax.nn.silu(r_q) * HGRN_DK ** -0.5, HGRN_HEADS), k_f, k_b, to_heads(r_i, HGRN_HEADS), logf_f, logf_b)
    return gla, hgrn, g_gate, r_gate

def gated_head_norm(o, gain, gate):
    o = o * lax.rsqrt(jnp.mean(jnp.square(o), axis=-1, keepdims=True) + NORM_EPS) * gain.astype(jnp.float32)
    return from_heads(o) * jax.nn.silu(gate.astype(jnp.float32))

def token_mixer(h, hc, with_ctx_output, w_in, a2_f, a2_b, a_bias_f, a_bias_b, lb_f, lb_b, gla_gain, hgrn_gain, w_out):
    gla, hgrn, gla_gate, hgrn_gate = mixer_features(h, w_in, a2_f, a2_b, a_bias_f, a_bias_b, lb_f, lb_b)
    gla_c, hgrn_c, gla_gate_c, hgrn_gate_c = mixer_features(hc, w_in, a2_f, a2_b, a_bias_f, a_bias_b, lb_f, lb_b)
    o_gla, oc_gla = bidirectional_scan(gla, gla_c)
    o_hgrn, oc_hgrn = bidirectional_scan(hgrn, hgrn_c)

    def project(o1, g1, o2, g2):
        merged = jnp.concatenate([gated_head_norm(o1, gla_gain, g1), gated_head_norm(o2, hgrn_gain, g2)], axis=-1)
        return merged.astype(w_out.dtype) @ w_out

    y = project(o_gla, gla_gate, o_hgrn, hgrn_gate)
    yc = project(oc_gla, gla_gate_c, oc_hgrn, hgrn_gate_c) if with_ctx_output else None
    return y, yc

def trunk_layer(x, xc, m, mc, update_ctx, ln_gain, ln_bias, ffn1_w_in, ffn1_w_out, w_mix_in,
                a2_f, a2_b, a_bias_f, a_bias_b, lb_f, lb_b, gla_gain, hgrn_gain, w_mix_out, ffn2_w_in, ffn2_w_out):
    x = residual_post_norm(x, swiglu(modulate(x, m, 0), ffn1_w_in, ffn1_w_out), m[:, 2], FFN_HALF, ln_gain[0], ln_bias[0])
    xc = residual_post_norm(xc, swiglu(modulate(xc, mc, 0), ffn1_w_in, ffn1_w_out), mc[:, 2], FFN_HALF, ln_gain[0], ln_bias[0])
    y, yc = token_mixer(modulate(x, m, 1), modulate(xc, mc, 1), update_ctx, w_mix_in, a2_f, a2_b, a_bias_f, a_bias_b,
                        lb_f, lb_b, gla_gain, hgrn_gain, w_mix_out)
    x = residual_post_norm(x, y, m[:, 5], 1.0, ln_gain[1], ln_bias[1])
    x = residual_post_norm(x, swiglu(modulate(x, m, 2), ffn2_w_in, ffn2_w_out), m[:, 8], FFN_HALF, ln_gain[2], ln_bias[2])
    if update_ctx:
        xc = residual_post_norm(xc, yc, mc[:, 5], 1.0, ln_gain[1], ln_bias[1])
        xc = residual_post_norm(xc, swiglu(modulate(xc, mc, 2), ffn2_w_in, ffn2_w_out), mc[:, 8], FFN_HALF, ln_gain[2], ln_bias[2])
    return x, xc

def setup_inputs(seed: int = 0) -> dict:
    key = jax.random.key(seed)
    ks = jax.random.split(key, 24)
    f32 = jnp.float32

    def w(k, shape, fan_in, scale=1.0):
        return jax.random.normal(k, shape, f32) * (scale * fan_in ** -0.5)

    def noise(k, shape, scale):
        return jax.random.normal(k, shape, f32) * scale

    n_mod = 3 * N_SUBLAYERS
    return {
        "x": jax.random.normal(ks[0], (BATCH, SEQ, D_MODEL), f32),
        "c": jax.random.normal(ks[1], (BATCH, D_MODEL), f32),
        "ctx": jax.random.normal(ks[2], (BATCH, CTX_LEN, D_MODEL), f32),
        "c_ctx": jax.random.normal(ks[3], (D_MODEL,), f32),
        "w_ada": w(ks[4], (DEPTH, D_MODEL, n_mod * D_MODEL), D_MODEL, 0.5),
        "b_ada": noise(ks[5], (DEPTH, n_mod * D_MODEL), 0.02),
        "ln_gain": 1.0 + noise(ks[6], (DEPTH, N_SUBLAYERS, D_MODEL), 0.05),
        "ln_bias": noise(ks[7], (DEPTH, N_SUBLAYERS, D_MODEL), 0.02),
        "ffn1_w_in": w(ks[8], (DEPTH, D_MODEL, 2 * D_FF), D_MODEL),
        "ffn1_w_out": w(ks[9], (DEPTH, D_FF, D_MODEL), D_FF, DN_BETA),
        "w_mix_in": w(ks[10], (DEPTH, D_MODEL, IN_WIDTH), D_MODEL),
        "gla_a2_fwd": w(ks[11], (DEPTH, GLA_GATE_RANK, GLA_QK), GLA_GATE_RANK),
        "gla_a2_bwd": w(ks[12], (DEPTH, GLA_GATE_RANK, GLA_QK), GLA_GATE_RANK),
        "gla_a_bias_fwd": noise(ks[13], (DEPTH, GLA_QK), 0.1),
        "gla_a_bias_bwd": noise(ks[14], (DEPTH, GLA_QK), 0.1),
        "hgrn_lb_logits": noise(ks[15], (2, DEPTH + 1, HGRN_K), 0.1),
        "gla_norm_gain": 1.0 + noise(ks[16], (DEPTH, GLA_DV), 0.05),
        "hgrn_norm_gain": 1.0 + noise(ks[17], (DEPTH, HGRN_DV), 0.05),
        "w_mix_out": w(ks[18], (DEPTH, MIX_WIDTH, D_MODEL), MIX_WIDTH, DN_BETA),
        "ffn2_w_in": w(ks[19], (DEPTH, D_MODEL, 2 * D_FF), D_MODEL),
        "ffn2_w_out": w(ks[20], (DEPTH, D_FF, D_MODEL), D_FF, DN_BETA),
    }

def reference(x, c, ctx, c_ctx, w_ada, b_ada, ln_gain, ln_bias, ffn1_w_in, ffn1_w_out, w_mix_in,
              gla_a2_fwd, gla_a2_bwd, gla_a_bias_fwd, gla_a_bias_bwd, hgrn_lb_logits,
              gla_norm_gain, hgrn_norm_gain, w_mix_out, ffn2_w_in, ffn2_w_out):
    bsz, n_tok, d = x.shape
    rows = n_tok // GRID_W
    x = x + sincos_2d(rows, GRID_W, d).astype(x.dtype)[None]
    xc = ctx
    lb = jnp.cumsum(jax.nn.softmax(hgrn_lb_logits.astype(jnp.float32), axis=1), axis=1)
    n_mod = 3 * N_SUBLAYERS
    for l in range(DEPTH):
        m = (jax.nn.silu(c) @ w_ada[l] + b_ada[l]).reshape(bsz, n_mod, d)
        mc = (jax.nn.silu(c_ctx) @ w_ada[l] + b_ada[l]).reshape(1, n_mod, d)
        x, xc = trunk_layer(x, xc, m, mc, l < DEPTH - 1, ln_gain[l], ln_bias[l], ffn1_w_in[l], ffn1_w_out[l], w_mix_in[l],
                            gla_a2_fwd[l], gla_a2_bwd[l], gla_a_bias_fwd[l], gla_a_bias_bwd[l], lb[0, l], lb[1, l],
                            gla_norm_gain[l], hgrn_norm_gain[l], w_mix_out[l], ffn2_w_in[l], ffn2_w_out[l])
    return x


_drawn_inputs = setup_inputs


def setup_inputs(seed=0):
    import zlib

    import numpy as np

    out = dict(_drawn_inputs(seed))
    spreads = {}
    factors = {'ctx': 7.275,
     'c_ctx': 8.0,
     'b_ada': 5.222,
     'gla_a2_fwd': 3.587,
     'gla_a_bias_fwd': 8.0,
     'gla_a_bias_bwd': 8.0,
     'hgrn_lb_logits': 8.0,
     'gla_norm_gain': 8.0,
     'hgrn_norm_gain': 8.0}
    for name, (base, spread) in spreads.items():
        noise = np.random.default_rng([zlib.crc32(name.encode()), seed]).standard_normal(out[name].shape)
        drawn = base * np.exp(spread * noise) if base else spread * noise
        out[name] = jnp.asarray(drawn.astype(out[name].dtype))
    for name, factor in factors.items():
        out[name] = (out[name] * factor).astype(out[name].dtype)
    return out
```

```python
from contextlib import ExitStack

import concourse.bass as bass
from concourse import mybir

F32 = mybir.dt.float32
F32R = mybir.dt.float32r
I32 = mybir.dt.int32
ALU = mybir.AluOpType
ACT = mybir.ActivationFunctionType

P = 128
D = 1024
KT = D // P
FF = 2816
CTX, SEQ = 256, 512
TOK = CTX + SEQ
TC, TL = CTX // P, SEQ // P
TT = TC + TL
CHUNK = 32
NCH = TOK // CHUNK
CPT = P // CHUNK
CC = CTX // CHUNK
LC = SEQ // CHUNK
ALPHA = 2.0 ** 0.25
GLA_PAIRS, HGRN_HEADS = 2, 4
C_GQ, C_GK, C_GV, C_GG, C_LR = 0, 256, 512, 1024, 1536
C_RQ, C_RFF, C_RFB, C_RI, C_RG = 1568, 2080, 2592, 3104, 3616
R_BADA, R_GBIAS, R_LB, R_GAIN, R_C = 0, 72, 76, 92, 94
N_ROWS = 110
SLOT = 8 * 256

FFN1_GROUPS = ((0, 3), (3, 3))
FFN1_PARTS = (12, 10)
FFN2_PARTS = (8, 8, 6)
ADA_FIRST = 11
ADA_BLOCKS = 36
SEED = 1


class Steps:

    def __init__(self, sem, names_gla, names_hgrn):
        self.sem, self.names = sem, {"G": list(names_gla), "H": list(names_hgrn)}
        self.turn = 0

    def at(self, group, name):
        kind, n = group
        base = 0 if kind == "G" else GLA_PAIRS * len(self.names["G"])
        return base + n * len(self.names[kind]) + (self.names[kind].index(name) + 1)

    def before(self, group):
        kind, n = group
        base = 0 if kind == "G" else GLA_PAIRS * len(self.names["G"])
        return base + n * len(self.names[kind])

    def start(self, group):
        self.kind, self.turn = group[0], 0

    def done(self, ins, name):
        assert self.names[self.kind][self.turn] == name, (self.names[self.kind][self.turn], name)
        self.turn += 1
        ins.then_inc(self.sem, 1)

    def end(self):
        assert self.turn == len(self.names[self.kind])


def heads_of(kind):
    return ((0, 0, 64), (1, 64, 64)) if kind == "G" else ((0, 0, 128),)


def scan_tiles(d):
    return list(range(TT)) if d == 0 else list(range(TC))[::-1] + list(range(TC, TT))[::-1]


def pe_names(kind):
    out = ["z0", "z1"] if kind == "G" else []
    out += [f"vT{i}" for i, _, _ in heads_of(kind)]
    out += ["T0"]
    for n in range(2 * TT):
        if n + 1 < 2 * TT:
            out.append(f"T{n + 1}")
        out.append(f"U{n}")
    for t in range(TL):
        for i, _, _ in heads_of(kind):
            out += [f"att{t}{i}0", f"att{t}{i}1", f"intra{t}{i}0", f"o{t}{i}"]
    out += [f"ms{i}" for i, _, _ in heads_of(kind)]
    return out


def act_names(kind):
    gating = lambda d: [f"eb{d}", f"einv{d}", f"dec{d}", f"tail{d}"]
    if kind == "H":
        out = ["sig0", "sig1", "ln0"] + gating(0) + ["ln1"] + gating(1)
        out += ["vf0", "sigq", "sigg0", "vt0a", "vt0b"]
    else:
        out = ["k", "q", "z0", "z1"]
        for d in range(2):
            out += [f"abs{d}", f"ex{d}", f"ln{d}"] + gating(d)
        out += ["vf0", "vt0a", "vt0b", "vf1", "vt1a", "vt1b", "sigg0", "sigg1"]
    out += [x for i, _, _ in heads_of(kind) for x in (f"sq{i}", f"lnms{i}", f"rinv{i}")]
    return out


def dve_names(kind):
    out = ["lb"] if kind == "H" else []
    for d in range(2):
        out += [f"f{d}", f"k{d}"] if kind == "H" else [f"zm{d}", f"g{d}"]
        out += [f"b{d}", f"diff{d}", f"kinv{d}", f"tail{d}"]
    out += ["q", "gate0"] if kind == "H" else ["gate0", "gate1"]
    out += ["qdec0", "qdec1"]
    for s in range(TT):
        out += [f"kt{2 * s}", f"kt{2 * s + 1}"]
        for c in range(CPT):
            for d in range(2):
                if s * CPT + c < NCH - 1:
                    out.append(f"S{d}_{s * CPT + c}")
    for t in range(TL):
        for i, _, _ in heads_of(kind):
            out += [f"am{t}{i}0", f"am{t}{i}1"]
    out += [x for i, _, _ in heads_of(kind) for x in (f"og{i}", f"on{i}", f"m{i}")]
    return out


def build(nc, t, out):
    with ExitStack() as ctx:
        def sb(name, shape, dt=F32, where=ctx):
            return where.enter_context(nc.sbuf_tensor(name, shape, dt))

        def sem(name):
            return ctx.enter_context(nc.semaphore(name))

        h_hi = sb("h_hi", [P, KT, TOK], F32R)
        h_lo = sb("h_lo", [P, KT, TOK], F32R)
        xtok = sb("xtok", [P, TT, D])
        w_raw = [sb(f"w_raw{s}", [P, SLOT]) for s in range(2)]
        w_hi = [sb(f"w_hi{s}", [P, SLOT], F32R) for s in range(2)]
        w_lo = [sb(f"w_lo{s}", [P, SLOT], F32R) for s in range(2)]
        work = sb("work", [P, 4 * D])
        gain_b, bias_b, xn = (work[:, i * D:(i + 1) * D] for i in range(3))
        hfull = work[:, 3 * D:4 * D].rearrange("p (k c) -> p k c", c=P)
        ident = sb("ident", [P, P])
        ones = sb("ones", [P, P])
        rows = sb("rows", [P, P])
        cols = sb("cols", [P, N_ROWS])
        mods = sb("mods", [P, 72, 2])
        scale1 = sb("scale1", [P, KT, 2])
        gate_w = sb("gate_w", [P, KT, 2])
        lb = sb("lb", [P, 2, HGRN_HEADS])
        lb1 = sb("lb1", [P, 2, HGRN_HEADS])
        small = sb("small", [P, 32])
        stats = sb("stats", [P, 12])
        mv = sb("mv", [P, 2])
        lnv = sb("lnv", [P, 1])
        rstd = sb("rstd", [P, 1])
        eps_ln = sb("eps_ln", [P, 1])
        eps_rms = sb("eps_rms", [P, 1])
        cmask = sb("cmask", [P, CPT])
        smask = sb("smask", [P, TOK], mybir.dt.bfloat16)
        amask = sb("amask", [P, 2, P], I32)
        attT = sb("attT", [P, 2, P])

        def ffn_set(where, tag, n_hidden, n):
            return (sb(f"hid_hi_{tag}", [P, n_hidden, n], F32R, where),
                    sb(f"hid_lo_{tag}", [P, n_hidden, n], F32R, where),
                    sb(f"yT_{tag}", [P, KT, n], F32, where),
                    sb(f"silu_{tag}", [P, 2, n], F32, where),
                    sb(f"hidden_{tag}", [P, 2, n], F32, where))

        n1, n2 = FFN1_GROUPS[0][1] * P, SEQ
        with ExitStack() as s1:
            ffn1 = ffn_set(s1, "ffn1", max(FFN1_PARTS), n1)
            w_ada = sb("ada_block", [P, KT, 256], F32, s1)
        with ExitStack() as s2:
            mT = sb("mT", [P, KT, SEQ], F32, s2)
            St = [sb(f"state{d}", [P, LC, P], F32, s2) for d in range(2)]
            qdec = [sb(f"qdec{d}", [P, SEQ], F32, s2) for d in range(2)]
            kinv = [sb(f"kinv{d}", [P, SEQ], F32, s2) for d in range(2)]
            tail = [sb(f"tail{d}", [P, TOK], F32, s2) for d in range(2)]
            vtok = [sb(f"vtok{i}", [P, TT, P], F32, s2) for i in range(2)]
            qf = sb("qf", [P, SEQ], F32, s2)
            gates = [sb(f"gate{i}", [P, SEQ], F32, s2) for i in range(2)]
            dec = [sb(f"dec{d}", [P, NCH], F32, s2) for d in range(2)]
            kt4 = [sb(f"kt4_{i}", [P, CPT, P], F32, s2) for i in range(2)]
            lbh = sb("lbh", [P, 2, 2], F32, s2)
        with ExitStack() as s3:
            ffn2 = ffn_set(s3, "ffn2", max(FFN2_PARTS), n2)
        T = [work[:, i * TOK:(i + 1) * TOK] for i in range(5)]
        ctx_part = xtok[:, 0:TC, :].rearrange("p a b -> p (a b)")
        lr = ctx_part[0:32, 0:TOK]
        a2 = [ctx_part[0:32, TOK + d * 256:TOK + (d + 1) * 256] for d in range(2)]
        vf = ctx_part[:, TOK + 512:2 * TOK + 512]
        yT1 = ffn1[2][:, :, :].rearrange("p k c -> p (k c)")
        prow = [yT1[:, i * 512:(i + 1) * 512] for i in range(TL)]
        pcol = yT1[:, TL * 512:(TL + 1) * 512]

        psA = ctx.enter_context(nc.psum_tensor("psA", [P, 4, 512], F32))
        psX = ctx.enter_context(nc.psum_tensor("psX", [P, 4, 512], F32))
        turn = psX[:, 0:2, :].rearrange("p a b -> p (a b)")
        ada_ps = psX[:, 2, 0:4].rearrange("p (a b) -> p a b", b=2)

        s_zero = sem("constants_set")
        s_const = sem("constants_loaded")
        s_x = sem("x_loaded")
        s_loaded = [sem(f"slot{s}_loaded") for s in range(2)]
        s_hi = [sem(f"slot{s}_hi_ready") for s in range(2)]
        s_lo = [sem(f"slot{s}_lo_ready") for s in range(2)]
        s_done = [sem(f"slot{s}_products_done") for s in range(2)]
        s_ada_loaded = sem("ada_loaded")
        s_ada_done = sem("ada_products_done")
        s_ada_out = sem("ada_evacuated")
        s_cols_ps = sem("cols_turned")
        s_cols = sem("cols_ready")
        s_silu_c = sem("silu_c_ready")
        s_lbe = sem("lb_exp_ready")
        s_own = sem("vector_chain")
        s_scale = sem("scale_ready")
        s_stat = sem("stats_ready")
        s_rstd = sem("rstd_ready")
        s_lnv = sem("ln_var_ready")
        s_xn = sem("xn_ready")
        s_turned = sem("x_turned")
        s_mod = sem("modulated")
        s_hhi = sem("h_hi_ready")
        s_h = sem("h_ready")
        s_ygate = sem("y_gated")
        s_yturned = sem("y_turned")
        s_r = sem("residual_summed")
        s_xnew = sem("x_updated")
        s_silu = sem("silu_ready")
        s_hf = sem("hidden_ready")
        s_hidhi = sem("hidden_hi_ready")
        s_hid = sem("hidden_split")
        s_y0 = sem("y_first_part")
        s_y1 = sem("y_later_part")
        s_gb = sem("gain_bias_loaded")
        s_a2 = sem("a2_loaded")
        s_a2z = sem("a2_zeroed")
        s_lr = sem("lr_ready")
        s_mask_turn = sem("mask_turns")
        s_mhi = sem("merged_hi_ready")
        s_m = sem("merged_split")
        s_mo = sem("mixer_out_evacuated")
        s_out = sem("output_stored")
        pes = Steps(sem("mixer_tensor_step"), pe_names("G"), pe_names("H"))
        acs = Steps(sem("mixer_scalar_step"), act_names("G"), act_names("H"))
        dvs = Steps(sem("mixer_vector_step"), dve_names("G"), dve_names("H"))

        ffn_phases = {}
        pair, n_in, n_out = 0, 0, 0
        for name, parts in (("A", FFN1_PARTS), ("B", FFN1_PARTS), ("mix", None), ("F", FFN2_PARTS)):
            if parts is None:
                mix_pair = pair
                mix_out_pair = pair + 2 * (GLA_PAIRS + HGRN_HEADS)
                pair = mix_out_pair + 2
                continue
            first, ph = 0, []
            for n in parts:
                ph.append((n, first, pair, pair + n // 2, n_in, n_out))
                pair += n // 2 + 4
                n_in += n // 2
                n_out += 4
                first += n
            ffn_phases[name] = ph
        last_pair = pair - 1
        y0_before, y1_before, y0_after, y1_after, y0_wait, y1_wait = {}, {}, {}, {}, {}, {}
        n0 = n_1 = 0
        for name in ("A", "B", "F"):
            ph = ffn_phases[name]
            for j, (_, _, p_in, p_out, _, _) in enumerate(ph):
                y0_after[p_in] = y0_after[p_out] = n0
                y1_before[p_in] = y1_before[p_out] = n_1
                y0_wait[p_out] = [max(n0 - 2 + 2 * u, 0) if j == 0 else n0 for u in range(2)]
                y1_wait[p_out] = [max(n_1 - 2 + 2 * u, 0) if j else n_1 for u in range(2)]
                y0_wait[p_out][0] = max(n0 - 2, 0)
                y1_wait[p_out][0] = max(n_1 - 2, 0)
                if j == 0:
                    n0 += KT
                else:
                    n_1 += KT
            y1_after[ph[0][2]] = n_1
        pre_jobs = ([(tt, 0) for tt in range(TT)] + [(tt, 1) for tt in range(TT)]
                    + [(tt, 2) for tt in range(TC, TT)])
        post_jobs = [(tt, 0) for tt in range(TT)] + [(tt, s) for s in (1, 2) for tt in range(TC, TT)]

        w1i = t["ffn1_w_in"].rearrange("(k p) n -> p k n", p=P)
        w1o = t["ffn1_w_out"].rearrange("(k p) n -> p k n", p=P)
        w2i = t["ffn2_w_in"].rearrange("(k p) n -> p k n", p=P)
        w2o = t["ffn2_w_out"].rearrange("(k p) n -> p k n", p=P)
        wmi = t["w_mix_in"].rearrange("(k p) n -> p k n", p=P)
        wmo = t["w_mix_out"].rearrange("(k p) n -> p k n", p=P)
        wad = t["w_ada"].rearrange("(k p) n -> p k n", p=P)

        def slot_view(buf, k, c):
            return buf[:, 0:k * c].rearrange("p (k c) -> p k c", c=c)

        def halves(k):
            return (0, (k + 1) // 2), ((k + 1) // 2, k)

        def mix_group_pair(g):
            return mix_pair + 2 * g[1] + (2 * GLA_PAIRS if g[0] == "H" else 0)

        block = ctx.enter_context(nc.Block())

        @block.sync
        def _(sp):
            def slot_free(s, p):
                sp.wait_ge(s_lo[s], p + SEED)

            def ada(b):
                if not (isinstance(b, int) and b == 0):
                    sp.wait_ge(s_ada_done, b)
                sp.dma_start(w_ada[:, :, :], wad[:, :, bass.ds(b * 256, 256)]).then_inc(s_ada_loaded, 16)

            def ffn_loads(phases, wi, wo, with_ada):
                for n, first, p_in, p_out, _, _ in phases:
                    with sp.Fori(p_in, p_in + n // 2) as p:
                        for s in range(2):
                            slot_free(s, p)
                            c0 = (first - 2 * p_in) * P + s * FF
                            for a, b in halves(KT):
                                sp.dma_start(slot_view(w_raw[s], KT, 256)[:, a:b, :],
                                             wi[:, a:b, bass.ds(p * 256 + c0, 256)]).then_inc(s_loaded[s], 16)
                        if with_ada(p_in):
                            ada(p + ADA_FIRST)
                    with sp.Fori(p_out, p_out + 4) as p:
                        for s in range(2):
                            slot_free(s, p)
                            k0 = first + s * (n // 2)
                            for a, b in halves(n // 2):
                                sp.dma_start(slot_view(w_raw[s], n // 2, 256)[:, a:b, :],
                                             wo[:, k0 + a:k0 + b, bass.ds(p * 256 - p_out * 256, 256)]
                                             ).then_inc(s_loaded[s], 16)
                        if with_ada(p_out):
                            ada(p + ADA_FIRST)

            def gain_bias(s):
                for dst, name in ((gain_b, "ln_gain"), (bias_b, "ln_bias")):
                    sp.dma_start(dst, t[name][s:s + 1, :].broadcast_to([P, D])).then_inc(s_gb, 16)

            sp.dma_start(rows[R_BADA:R_BADA + 72, :], t["b_ada"]).then_inc(s_const, 16)
            sp.dma_start(rows[R_GBIAS:R_GBIAS + 2, :], t["gla_a_bias_fwd"]).then_inc(s_const, 16)
            sp.dma_start(rows[R_GBIAS + 2:R_GBIAS + 4, :], t["gla_a_bias_bwd"]).then_inc(s_const, 16)
            sp.dma_start(rows[R_LB:R_LB + 16, :], t["hgrn_lb_logits"]).then_inc(s_const, 16)
            sp.dma_start(rows[R_GAIN:R_GAIN + 1, :], t["gla_norm_gain"]).then_inc(s_const, 16)
            sp.dma_start(rows[R_GAIN + 1:R_GAIN + 2, :], t["hgrn_norm_gain"]).then_inc(s_const, 16)
            sp.dma_start(rows[R_C:R_C + 8, :], t["c"]).then_inc(s_const, 16)
            sp.dma_start(rows[R_C + 8:R_C + 16, :], t["c_ctx"]).then_inc(s_const, 16)
            sp.dma_start(ident[:, :], t["k_ident"]).then_inc(s_const, 16)
            sp.dma_start(ones[:, :], t["k_ones"]).then_inc(s_const, 16)
            sp.dma_start(cmask[:, :], t["k_cmask"]).then_inc(s_const, 16)
            sp.dma_start(smask[:, :], t["k_smask"]).then_inc(s_const, 16)
            sp.dma_start(amask[:, :, :], t["k_amask"]).then_inc(s_const, 16)
            ada(0)
            for tt in range(TC):
                sp.dma_start(xtok[:, tt, :], t["ctx"][tt * P:(tt + 1) * P, :]).then_inc(s_x, 16)
            for i in range(TL):
                sp.dma_start(xtok[:, TC + i, :], t["x"][i * P:(i + 1) * P, :]).then_inc(s_x, 16)
                for r in range(2):
                    sp.dma_start(prow[i][r * 64:(r + 1) * 64, :],
                                 t["k_prow"][2 * i + r:2 * i + r + 1, :].broadcast_to([64, 512])).then_inc(s_x, 16)
            sp.dma_start(pcol, t["k_pcol"]).then_inc(s_x, 16)
            for b in range(1, ADA_FIRST):
                ada(b)
            gain_bias(0)
            ffn_loads(ffn_phases["A"], w1i, w1o, lambda p: True)
            ffn_loads(ffn_phases["B"], w1i, w1o, lambda p: p + ADA_FIRST < ADA_BLOCKS)

            def mix_slot(s, p, *pieces):
                slot_free(s, p)
                if len(pieces) == 2:
                    for i, c0 in enumerate(pieces):
                        sp.dma_start(slot_view(w_raw[s], 2 * KT, P)[:, i * KT:(i + 1) * KT, :],
                                     wmi[:, :, bass.ds(c0, P)]).then_inc(s_loaded[s], 16)
                    return
                (c0, width), = pieces
                for a, b in halves(KT):
                    sp.dma_start(slot_view(w_raw[s], KT, width)[:, a:b, :],
                                 wmi[:, a:b, bass.ds(c0, width)]).then_inc(s_loaded[s], 16)

            for pr in range(GLA_PAIRS):
                p = mix_group_pair(("G", pr))
                if pr == 0:
                    mix_slot(0, p, C_GK, C_GQ)
                    mix_slot(1, p, (C_LR, 32))
                else:
                    mix_slot(0, p, (C_GK + P * pr, P))
                    mix_slot(1, p, (C_GQ + P * pr, P))
                mix_slot(0, p + 1, (C_GV + 2 * P * pr, 2 * P))
                mix_slot(1, p + 1, (C_GG + 2 * P * pr, 2 * P))
            with sp.Fori(0, HGRN_HEADS) as h:
                p = mix_group_pair(("H", h))
                mix_slot(0, p, (h * P + C_RFF, P))
                mix_slot(1, p, (h * P + C_RFB, P))
                mix_slot(0, p + 1, (h * P + C_RI, P))
                mix_slot(1, p + 1, h * P + C_RQ, h * P + C_RG)
            for i in range(2):
                p = mix_out_pair + i
                for s in range(2):
                    slot_free(s, p)
                    for a, b in halves(KT):
                        sp.dma_start(slot_view(w_raw[s], KT, 256)[:, a:b, :],
                                     wmo[:, a:b, (2 * i + s) * 256:(2 * i + s + 1) * 256]).then_inc(s_loaded[s], 16)
            sp.wait_ge(dvs.sem, dvs.before(("H", HGRN_HEADS)))
            gain_bias(1)
            ffn_loads(ffn_phases["F"], w2i, w2o, lambda p: False)
            sp.wait_ge(s_xnew, TT + TL)
            gain_bias(2)
            for i in range(TL):
                sp.wait_ge(s_xnew, TT + TL + i + 1)
                sp.dma_start(out[i * P:(i + 1) * P, :], xtok[:, TC + i, :]).then_inc(s_out, 16)
            sp.wait_ge(s_out, 16 * TL)

        @block.gpsimd
        def _(pool):
            nc.gpsimd.memset(attT[:, :, :], 0.0).then_inc(s_zero, 1)
            nc.gpsimd.memset(eps_ln[:, :], 1e-5).then_inc(s_zero, 1)
            nc.gpsimd.memset(eps_rms[:, :], 1e-6).then_inc(s_zero, 1)
            pool.wait_ge(s_xn, 2 * TT)
            nc.gpsimd.memset(ctx_part[0:32, TOK:TOK + 512], 0.0).then_inc(s_a2z, 1)
            pool.wait_ge(s_a2z, 1)
            pool.dma_start(a2[0][0:16, :], t["gla_a2_fwd"]).then_inc(s_a2, 16)
            pool.dma_start(a2[1][16:32, :], t["gla_a2_bwd"]).then_inc(s_a2, 16)

        @block.scalar
        def _(act):
            def split_hi(s, p):
                act.wait_ge(s_loaded[s], p * 32 + 32)
                act.wait_ge(s_lo[s], p + SEED)
                act.wait_ge(s_done[s], p)
                nc.scalar.activation(w_hi[s][:, :], w_raw[s][:, :], ACT.Copy).then_inc(s_hi[s], 1)

            n_stat = [0]

            def rstd_of():
                n_stat[0] += 1
                act.wait_ge(s_stat, n_stat[0])
                nc.scalar.activation(lnv[:, :], mv[:, 1:2], ACT.Ln, bias=eps_ln[:, :]).then_inc(s_lnv, 1)
                act.wait_ge(s_lnv, n_stat[0])
                nc.scalar.activation(rstd[:, :], lnv[:, :], ACT.Exp, scale=-0.5).then_inc(s_rstd, 1)

            def pre(q):
                tt, s = pre_jobs[q]
                v = 1 if tt < TC else 0
                rstd_of()
                act.wait_ge(s_scale, (1, 3, 5)[s])
                act.wait_ge(s_turned, q + 1)
                act.wait_ge(s_h, q)
                act.wait_ge(s_hhi, q)
                for k in range(KT):
                    ins = nc.scalar.activation(hfull[:, k, :], turn[:, k * P:(k + 1) * P], ACT.Identity,
                                               bias=mods[:, (3 * s + 1) * KT + k, v:v + 1],
                                               scale=scale1[:, k, v:v + 1])
                ins.then_inc(s_mod, 1)
                act.wait_ge(s_mod, q + 1)
                nc.scalar.activation(h_hi[:, :, tt * P:(tt + 1) * P], hfull, ACT.Copy).then_inc(s_hhi, 1)

            def post(q):
                rstd_of()

            def ffn(phases, bufs, n, gate_count, gated, segs):
                hid_hi, _, yT, sg, hf = bufs
                for j, (tiles, _, p_in, p_out, i0, _) in enumerate(phases):
                    with act.Fori(0, tiles // 2) as i:
                        p = i + p_in
                        act.wait_ge(s_done[0], p + 1)
                        split_hi(0, p + 1)
                        act.wait_ge(s_hf, i * 2 + 2 * i0 + SEED)
                        for u in range(2):
                            nc.scalar.activation(sg[:, u, :], psA[:, u, 0:n], ACT.Silu).then_inc(s_silu, 1)
                        act.wait_ge(s_done[1], p + 1)
                        split_hi(1, p + 1)
                        for u in range(2):
                            act.wait_ge(s_hf, i * 2 + (2 * i0 + u + 1) + SEED)
                            nc.scalar.activation(hid_hi[:, bass.ds(i * 2 + u, 1), :], hf[:, u:u + 1, :],
                                                 ACT.Copy).then_inc(s_hidhi, 1)

                    def out_pair(p, u, d):
                        act.wait_ge(s_done[0], p + 1)
                        split_hi(0, p + 1)
                        act.wait_ge(s_done[1], p + 1)
                        if j == 0:
                            for v in range(2):
                                nc.scalar.activation(yT[:, bass.ds(d + v, 1), :], psA[:, 2 * u + v:2 * u + v + 1, 0:n],
                                                     ACT.Copy).then_inc(s_y0, 1)

                    last = p_out + 3 == last_pair
                    if not last:
                        with act.Fori(0, 2) as hh:
                            for u in range(2):
                                p = hh * 2 + (p_out + u)
                                out_pair(p, u, hh * 4 + 2 * u)
                                split_hi(1, p + 1)
                    else:
                        for o in range(3):
                            out_pair(p_out + o, o % 2, 2 * o)
                            split_hi(1, p_out + o + 1)
                act.wait_ge(s_scale, gate_count)
                act.wait_ge(s_y1, y1_after[phases[0][2]] + SEED)
                for k in range(KT):
                    for v, a, b in segs:
                        ins = nc.scalar.activation(yT[:, k, a:b], yT[:, k, a:b], ACT.Copy,
                                                   scale=gate_w[:, k, v:v + 1])
                ins.then_inc(s_ygate, 1)

            for ring in (s_silu, s_y0):
                act.sem_inc(ring, SEED)
            act.wait_ge(s_cols, 1)
            nc.scalar.activation(small[:, 0:16], cols[:, R_C:R_C + 16], ACT.Silu).then_inc(s_silu_c, 1)
            act.wait_ge(s_own, 2)
            nc.scalar.activation(small[:, 16:32], small[:, 16:32], ACT.Exp).then_inc(s_lbe, 1)
            act.wait_ge(s_zero, 3)
            for q in range(TT):
                pre(q)
            for s in range(2):
                split_hi(s, 0)
            for g, (t0, nt) in enumerate(FFN1_GROUPS):
                segs = [(1, 0, TC * P), (0, TC * P, n1)] if g == 0 else [(0, 0, n1)]
                ffn(ffn_phases["AB"[g]], ffn1, n1, 2, g + 1, segs)
                for q in range(t0, t0 + nt):
                    post(q)
                    pre(TT + q)

            def mixer(g):
                kind, _ = g
                acs.start(g)
                p = mix_group_pair(g)
                prev = lambda: (act.wait_ge(dvs.sem, dvs.before(g)), act.wait_ge(pes.sem, pes.before(g)))

                def wait_self(name):
                    act.wait_ge(acs.sem, acs.at(g, name))

                def wait_dve(name):
                    act.wait_ge(dvs.sem, dvs.at(g, name))

                def wait_pe(name):
                    act.wait_ge(pes.sem, pes.at(g, name))

                def gating(d, s):
                    lat = slice(TC * P, TOK)
                    edge = CHUNK - 1 if d == 0 else 0
                    wait_dve(f"b{d}")
                    acs.done(nc.scalar.activation(qdec[d][:, :], T[4][:, lat], ACT.Exp, scale=s), f"eb{d}")
                    acs.done(nc.scalar.activation(T[0][:, lat], T[4][:, lat], ACT.Exp, scale=-s), f"einv{d}")
                    acs.done(nc.scalar.activation(
                        dec[d][:, :], T[4].rearrange("p (n c) -> p n c", c=CHUNK)[:, :, edge], ACT.Exp, scale=s),
                        f"dec{d}")
                    wait_dve(f"diff{d}")
                    acs.done(nc.scalar.activation(T[3], T[3], ACT.Exp, scale=s), f"tail{d}")

                prev()
                if kind == "G":
                    pr = g[1]
                    act.wait_ge(s_done[0], p + 1)
                    split_hi(0, p + 1)
                    acs.done(nc.scalar.activation(T[1][:, 0:2 * n1].rearrange("p (a b) -> p a b", b=n1),
                                                  psA[:, 0:2, 0:n1], ACT.Copy), "k")
                    act.wait_ge(s_done[1], p + 1)
                    acs.done(nc.scalar.activation(qf[:, :], psA[:, 2, :], ACT.Copy, scale=64.0 ** -0.5), "q")
                    if pr == 0:
                        nc.scalar.activation(lr.rearrange("p (a b) -> p a b", b=n1), psX[0:32, 0:2, 0:n1],
                                             ACT.Copy).then_inc(s_lr, 1)
                    split_hi(1, p + 1)
                    for d in range(2):
                        wait_pe(f"z{d}")
                        dst = T[0] if d == 0 else tail[1][:, :]
                        b0 = R_GBIAS + 2 * d + pr
                        acs.done(nc.scalar.activation(dst.rearrange("p (a b) -> p a b", b=n1),
                                                      psX[:, 2 * d:2 * d + 2, 0:n1], ACT.Identity,
                                                      bias=cols[:, b0:b0 + 1]), f"z{d}")
                    for d in range(2):
                        wait_self(f"z{d}")
                        z = T[0] if d == 0 else tail[1][:, :]
                        if d == 1:
                            wait_self("tail0")
                            wait_dve("tail0")
                        acs.done(nc.scalar.activation(T[2], z, ACT.Abs), f"abs{d}")
                        wait_self(f"abs{d}")
                        acs.done(nc.scalar.activation(T[2], T[2], ACT.Exp, scale=-1.0), f"ex{d}")
                        wait_self(f"ex{d}")
                        acs.done(nc.scalar.activation(T[2], T[2], ACT.Ln, bias=1.0), f"ln{d}")
                        gating(d, 1.0 / 16.0)
                else:
                    act.wait_ge(s_done[0], p + 1)
                    split_hi(0, p + 1)
                    acs.done(nc.scalar.activation(T[0].rearrange("p (a b) -> p a b", b=n1),
                                                  psA[:, 0:2, 0:n1], ACT.Sigmoid), "sig0")
                    act.wait_ge(s_done[1], p + 1)
                    split_hi(1, p + 1)
                    acs.done(nc.scalar.activation(tail[1][:, :].rearrange("p (a b) -> p a b", b=n1),
                                                  psA[:, 2:4, 0:n1], ACT.Sigmoid), "sig1")
                    for d in range(2):
                        wait_dve(f"f{d}")
                        acs.done(nc.scalar.activation(T[3], T[0], ACT.Ln), f"ln{d}")
                        gating(d, 1.0)
                for i, _, _ in heads_of(kind):
                    act.wait_ge(s_done[0], p + 2)
                    src = psX[:, 0:2, 0:n1] if kind == "H" else psA[:, 2 * i:2 * i + 2, 0:n1]
                    if i == 1:
                        wait_pe("vT0")
                    acs.done(nc.scalar.activation(vf.rearrange("p (a b) -> p a b", b=n1), src, ACT.Copy), f"vf{i}")
                    if i == 0:
                        split_hi(0, p + 2)
                        act.wait_ge(s_done[1], p + 2)
                        if kind == "H":
                            acs.done(nc.scalar.activation(qf[:, :], psX[:, 2, :], ACT.Sigmoid), "sigq")
                            acs.done(nc.scalar.activation(gates[0][:, :], psX[:, 3, :], ACT.Sigmoid), "sigg0")
                        split_hi(1, p + 2)
                    wait_pe(f"vT{i}")
                    acs.done(nc.scalar.activation(vtok[i][:, 0:4, :], psX[:, 0, :].rearrange("p (a b) -> p a b", b=P),
                                                  ACT.Copy), f"vt{i}a")
                    acs.done(nc.scalar.activation(vtok[i][:, 4:6, :],
                                                  psX[:, 1, 0:2 * P].rearrange("p (a b) -> p a b", b=P),
                                                  ACT.Copy), f"vt{i}b")
                if kind == "G":
                    for i in range(2):
                        acs.done(nc.scalar.activation(gates[i][:, :], psX[:, 2 + i, :], ACT.Sigmoid), f"sigg{i}")
                for i, _, _ in heads_of(kind):
                    wait_pe(f"o{TL - 1}{i}")
                    if i == 1:
                        wait_pe("ms0")
                    acs.done(nc.scalar.activation(T[0][:, 0:SEQ], psX[:, 2 + i, :], ACT.Square), f"sq{i}")
                    wait_pe(f"ms{i}")
                    if i == 1:
                        wait_dve("on0")
                    acs.done(nc.scalar.activation(T[2][:, 0:SEQ], psA[:, i, :], ACT.Ln, bias=eps_rms[:, :],
                                                  scale=1.0 / P), f"lnms{i}")
                    wait_self(f"lnms{i}")
                    acs.done(nc.scalar.activation(T[3][:, 0:SEQ], T[2][:, 0:SEQ], ACT.Exp, scale=-0.5), f"rinv{i}")
                acs.end()

            for pr in range(GLA_PAIRS):
                mixer(("G", pr))
            with act.Fori(0, HGRN_HEADS) as h:
                mixer(("H", h))

            act.wait_ge(dvs.sem, dvs.before(("H", HGRN_HEADS)))
            for k in range(KT):
                nc.scalar.activation(h_hi[:, k, TC * P:TOK], mT[:, k, :], ACT.Copy).then_inc(s_mhi, 1)
            act.wait_ge(s_m, KT)
            act.wait_ge(s_scale, 4)
            for i in range(2):
                p = mix_out_pair + i
                for s in range(2):
                    act.wait_ge(s_done[s], p + 1)
                    split_hi(s, p + 1)
                    for u in range(2):
                        d = 4 * i + 2 * s + u
                        nc.scalar.activation(mT[:, d, :], psA[:, 2 * s + u, :], ACT.Copy,
                                             scale=gate_w[:, d, 0:1]).then_inc(s_mo, 1)
            for q in range(TT, TT + TL):
                post(q)
                pre(2 * TT + q - TT)
            ffn(ffn_phases["F"], ffn2, n2, 6, 3, [(0, 0, n2)])
            for q in range(TT + TL, TT + 2 * TL):
                post(q)

        @block.vector
        def _(dve):
            own = [0]

            def link(ins):
                own[0] += 1
                ins.then_inc(s_own, 1)
                dve.wait_ge(s_own, own[0])

            def split_lo(s, p):
                dve.wait_ge(s_hi[s], p + 1)
                nc.vector.tensor_tensor(w_lo[s][:, :], w_raw[s][:, :], w_hi[s][:, :].bitcast(F32),
                                        ALU.subtract).then_inc(s_lo[s], 1)

            def ada_out(b):
                dve.wait_ge(s_ada_done, b + 1)
                bias = cols[:, bass.ds(b * 2, 2)].unsqueeze(2).to_broadcast([P, 2, 2])
                nc.vector.tensor_tensor(mods[:, bass.ds(b * 2, 2), :], ada_ps, bias, ALU.add).then_inc(s_ada_out, 1)

            n_stat = [0]

            def normalize(src, dst, done):
                for i in range(2):
                    ins = nc.vector.bn_stats(stats[:, 6 * i:6 * i + 6], src[:, i * 512:(i + 1) * 512])
                link(ins)
                n_stat[0] += 1
                nc.vector.bn_aggr(mv[:, :], stats[:, :]).then_inc(s_stat, 1)
                dve.wait_ge(s_rstd, n_stat[0])
                dve.wait_ge(s_stat, n_stat[0])
                done(nc.vector.tensor_scalar(dst, src, mv[:, 0:1], rstd[:, 0:1], ALU.subtract, ALU.mult))

            def pre(q):
                tt, s = pre_jobs[q]
                if q:
                    dve.wait_ge(s_turned, q)
                normalize(xtok[:, tt, :], xn, lambda ins: ins.then_inc(s_xn, 1))
                dve.wait_ge(s_hhi, q + 1)
                nc.vector.tensor_tensor(h_lo[:, :, tt * P:(tt + 1) * P], hfull,
                                        h_hi[:, :, tt * P:(tt + 1) * P].bitcast(F32), ALU.subtract).then_inc(s_h, 1)

            def post(q):
                tt, s = post_jobs[q]
                x = xtok[:, tt, :]
                dve.wait_ge(s_yturned, q + 1)
                ins = nc.vector.scalar_tensor_tensor(out=x, in0=x, scalar=ALPHA, in1=turn, op0=ALU.mult, op1=ALU.add)
                ins.then_inc(s_r, 1)
                dve.wait_ge(s_r, q + 1)
                normalize(x, x, link)
                dve.wait_ge(s_gb, 32 * (s + 1))
                link(nc.vector.tensor_tensor(x, x, gain_b, ALU.mult))
                nc.vector.tensor_tensor(x, x, bias_b, ALU.add).then_inc(s_xnew, 1)
                dve.wait_ge(s_xnew, q + 1)

            def scale_of(s):
                dve.wait_ge(s_ada_out, min(12 * s + 8, ADA_BLOCKS))
                dve.wait_ge(s_mod, (0, TT, 2 * TT)[s])
                nc.vector.tensor_scalar(scale1[:, :, :], mods[:, 24 * s:24 * s + 8, :], 1.0, None,
                                        ALU.add).then_inc(s_scale, 1)

            def gate_of(s):
                dve.wait_ge(s_ada_out, 12 * s + 12)
                nc.vector.tensor_scalar(gate_w[:, :, :], mods[:, 24 * s + 16:24 * s + 24, :],
                                        1.0 if s == 1 else 0.5, None, ALU.mult).then_inc(s_scale, 1)

            def ffn(phases, bufs, n, with_ada):
                hid_hi, hid_lo, yT, sg, hf = bufs
                for j, (tiles, _, p_in, p_out, i0, _) in enumerate(phases):
                    with dve.Fori(0, tiles // 2) as i:
                        p = i + p_in
                        split_lo(0, p + 1)
                        dve.wait_ge(s_done[1], p + 1)
                        dve.wait_ge(s_hid, i * 2 + 2 * i0 + SEED)
                        for u in range(2):
                            dve.wait_ge(s_silu, i * 2 + (2 * i0 + u + 1) + SEED)
                            nc.vector.tensor_tensor(hf[:, u, :], psA[:, 2 + u, 0:n], sg[:, u, :],
                                                    ALU.mult).then_inc(s_hf, 1)
                        split_lo(1, p + 1)
                        for u in range(2):
                            dve.wait_ge(s_hidhi, i * 2 + (2 * i0 + u + 1))
                            nc.vector.tensor_tensor(hid_lo[:, bass.ds(i * 2 + u, 1), :], hf[:, u:u + 1, :],
                                                    hid_hi[:, bass.ds(i * 2 + u, 1), :].bitcast(F32),
                                                    ALU.subtract).then_inc(s_hid, 1)
                        if with_ada(p_in):
                            ada_out(p + ADA_FIRST)

                    def out_pair(p, u, d):
                        split_lo(0, p + 1)
                        dve.wait_ge(s_done[1], p + 1)
                        if j:
                            for v in range(2):
                                y = yT[:, bass.ds(d + v, 1), :]
                                nc.vector.tensor_tensor(y, psA[:, 2 * u + v:2 * u + v + 1, 0:n], y,
                                                        ALU.add).then_inc(s_y1, 1)

                    if j:
                        dve.wait_ge(s_y0, y0_after[p_out] + SEED)
                        dve.wait_ge(s_y1, y1_before[p_out] + SEED)
                    if p_out + 3 == last_pair:
                        for o in range(3):
                            out_pair(p_out + o, o % 2, 2 * o)
                            split_lo(1, p_out + o + 1)
                        dve.wait_ge(s_done[1], p_out + 4)
                        for v in range(2):
                            y = yT[:, 6 + v:7 + v, :]
                            nc.vector.tensor_tensor(y, psA[:, 2 + v:3 + v, 0:n], y, ALU.add).then_inc(s_y1, 1)
                    else:
                        with dve.Fori(0, 2) as hh:
                            for u in range(2):
                                p = hh * 2 + (p_out + u)
                                out_pair(p, u, hh * 4 + 2 * u)
                                split_lo(1, p + 1)
                                if with_ada(p_out):
                                    ada_out(p + ADA_FIRST)

            for ring in (s_lo[0], s_lo[1], s_hf, s_hid, s_y1):
                dve.sem_inc(ring, SEED)
            dve.wait_ge(s_cols_ps, 1)
            nc.vector.tensor_copy(cols[:, :], psX[:, 3, 0:N_ROWS]).then_inc(s_cols, 1)
            dve.wait_ge(s_cols, 1)
            lg = cols[:, R_LB:R_LB + 16].rearrange("p (d l h) -> p d l h", d=2, l=2)
            ex = small[:, 16:32].rearrange("p (d l h) -> p d l h", d=2, l=2)
            link(nc.vector.tensor_tensor(lb[:, :, :], lg[:, :, 0, :], lg[:, :, 1, :], ALU.max))
            for l in range(2):
                ins = nc.vector.tensor_tensor(ex[:, :, l, :], lg[:, :, l, :], lb[:, :, :], ALU.subtract)
            link(ins)
            dve.wait_ge(s_lbe, 1)
            link(nc.vector.tensor_tensor(lb1[:, :, :], ex[:, :, 0, :], ex[:, :, 1, :], ALU.add))
            link(nc.vector.reciprocal(lb1[:, :, :], lb1[:, :, :]))
            link(nc.vector.tensor_tensor(lb[:, :, :], ex[:, :, 0, :], lb1[:, :, :], ALU.mult))
            link(nc.vector.tensor_scalar(lb1[:, :, :], lb[:, :, :], -1.0, 1.0, ALU.mult, ALU.add))
            dve.wait_ge(s_x, 16 * (TT + 2 * TL + 1))
            for i in range(TL):
                x = xtok[:, TC + i, :]
                nc.vector.tensor_tensor(x[:, 0:512], x[:, 0:512], prow[i], ALU.add)
                ins = nc.vector.tensor_tensor(x[:, 512:D], x[:, 512:D], pcol, ALU.add)
            link(ins)
            for b in range(ADA_FIRST):
                ada_out(b)
            scale_of(0)
            for q in range(TT):
                pre(q)
            for s in range(2):
                split_lo(s, 0)
            for g, (t0, nt) in enumerate(FFN1_GROUPS):
                ffn(ffn_phases["AB"[g]], ffn1, n1,
                    (lambda p: True) if g == 0 else (lambda p: p + ADA_FIRST < ADA_BLOCKS))
                if g == 0:
                    gate_of(0)
                    scale_of(1)
                for q in range(t0, t0 + nt):
                    post(q)
                    pre(TT + q)

            def mixer(g):
                kind, n = g
                dvs.start(g)
                p = mix_group_pair(g)

                def wait_self(name):
                    dve.wait_ge(dvs.sem, dvs.at(g, name))

                def wait_act(name):
                    dve.wait_ge(acs.sem, acs.at(g, name))

                def wait_pe(name):
                    dve.wait_ge(pes.sem, pes.at(g, name))

                dve.wait_ge(dvs.sem, dvs.before(g))
                dve.wait_ge(pes.sem, pes.before(g))
                dve.wait_ge(acs.sem, acs.before(g))
                if kind == "H":
                    nc.vector.tensor_copy(lbh[:, 0, :], lb[:, :, bass.ds(n, 1)].rearrange("p a b -> p (a b)"))
                    dvs.done(nc.vector.tensor_copy(lbh[:, 1, :], lb1[:, :, bass.ds(n, 1)].rearrange("p a b -> p (a b)")),
                             "lb")
                    wait_self("lb")
                split_lo(0, p + 1)
                split_lo(1, p + 1)
                for d in range(2):
                    lat = slice(TC * P, TOK)
                    edge = CHUNK - 1 if d == 0 else 0
                    if kind == "H":
                        wait_act(f"sig{d}")
                        if d == 1:
                            wait_act("tail0")
                            wait_self("tail0")
                        src = T[0] if d == 0 else tail[1][:, :]
                        dvs.done(nc.vector.tensor_scalar(T[0], src, lbh[:, 1, d:d + 1], lbh[:, 0, d:d + 1],
                                                         ALU.mult, ALU.add), f"f{d}")
                        wait_self(f"f{d}")
                        dvs.done(nc.vector.tensor_scalar(T[1], T[0], -1.0, 1.0, ALU.mult, ALU.add), f"k{d}")
                        wait_act(f"ln{d}")
                    else:
                        wait_act(f"z{d}")
                        if d == 1:
                            wait_act("tail0")
                            wait_self("tail0")
                        src = T[0] if d == 0 else tail[1][:, :]
                        dvs.done(nc.vector.tensor_scalar(T[3], src, 0.0, None, ALU.min), f"zm{d}")
                        wait_self(f"zm{d}")
                        wait_act(f"ln{d}")
                        dvs.done(nc.vector.tensor_tensor(T[3], T[3], T[2], ALU.subtract), f"g{d}")
                        wait_self(f"g{d}")
                    lf, b = (T[3], T[4]) if d == 0 else (T[3][:, ::-1], T[4][:, ::-1])
                    dvs.done(nc.vector.tensor_tensor_scan(b, smask[:, :], lf, 0.0, ALU.mult, ALU.add), f"b{d}")
                    wait_self(f"b{d}")
                    b3 = T[4].rearrange("p (n c) -> p n c", c=CHUNK)
                    dvs.done(nc.vector.tensor_tensor(
                        T[3].rearrange("p (n c) -> p n c", c=CHUNK),
                        b3[:, :, edge:edge + 1].to_broadcast([P, NCH, CHUNK]), b3, ALU.subtract), f"diff{d}")
                    wait_act(f"einv{d}")
                    dvs.done(nc.vector.tensor_tensor(kinv[d][:, :], T[1][:, lat], T[0][:, lat], ALU.mult), f"kinv{d}")
                    wait_act(f"tail{d}")
                    dvs.done(nc.vector.tensor_tensor(tail[d][:, :], T[1], T[3], ALU.mult), f"tail{d}")
                split_lo(0, p + 2)
                if kind == "H":
                    wait_act("sigg0")
                    dvs.done(nc.vector.scalar_tensor_tensor(out=qf[:, :], in0=qf[:, :], scalar=128.0 ** -0.5,
                                                            in1=psX[:, 2, :], op0=ALU.mult, op1=ALU.mult), "q")
                    dvs.done(nc.vector.tensor_tensor(gates[0][:, :], gates[0][:, :], psX[:, 3, :], ALU.mult), "gate0")
                    wait_self("q")
                else:
                    for i in range(2):
                        wait_act(f"sigg{i}")
                        dvs.done(nc.vector.tensor_tensor(gates[i][:, :], gates[i][:, :], psX[:, 2 + i, :], ALU.mult),
                                 f"gate{i}")
                for d in range(2):
                    dvs.done(nc.vector.tensor_tensor(qdec[d][:, :], qf[:, :], qdec[d][:, :], ALU.mult), f"qdec{d}")
                split_lo(1, p + 2)
                for s in range(TT):
                    for d in range(2):
                        m = 2 * s + d
                        wait_pe(f"T{m}")
                        if m >= 2:
                            wait_pe(f"U{m - 2}")
                        dvs.done(nc.vector.tensor_tensor(
                            kt4[d][:, :, :], psX[:, d, 0:P].unsqueeze(1).to_broadcast([P, CPT, P]),
                            cmask[:, :].unsqueeze(2).to_broadcast([P, CPT, P]), ALU.mult), f"kt{m}")
                    for c in range(CPT):
                        j = s * CPT + c
                        for d in range(2):
                            if j >= NCH - 1:
                                continue
                            if c == 0:
                                wait_pe(f"U{2 * s + d}")
                            lc = c if d == 0 else CPT - 1 - c
                            ch = scan_tiles(d)[s] * CPT + lc
                            u = psA[:, d, lc * P:(lc + 1) * P]
                            new = CC - 1 - j if j < CC else j - CC + 1
                            old = CC - j if j < CC else j - CC
                            if j == 0:
                                ins = nc.vector.tensor_copy(St[d][:, new, :], u)
                            else:
                                wait_self(f"S{d}_{j - 1}")
                                ins = nc.vector.scalar_tensor_tensor(
                                    out=St[d][:, new, :], in0=St[d][:, old, :], scalar=dec[d][:, ch:ch + 1],
                                    in1=u, op0=ALU.mult, op1=ALU.add)
                            dvs.done(ins, f"S{d}_{j}")
                for tt in range(TL):
                    for i, _, _ in heads_of(kind):
                        for d in range(2):
                            wait_pe(f"att{tt}{i}{d}")
                            seq = [(a, b) for a in range(TL) for b, _, _ in heads_of(kind)]
                            at = seq.index((tt, i))
                            if at:
                                pt, pi = seq[at - 1]
                                wait_pe(f"intra{pt}{pi}0" if d == 0 else f"o{pt}{pi}")
                                wait_self(f"am{pt}{pi}{d}")
                            dve.sem_inc(s_mask_turn, 1)
                            dvs.done(nc.vector.copy_predicated(attT[:, d, :], amask[:, d, :],
                                                               psA[:, 2 + d, 0:P]), f"am{tt}{i}{d}")
                for i, _, _ in heads_of(kind):
                    gcol = R_GAIN if kind == "G" else R_GAIN + 1
                    wait_act(f"sq{i}")
                    if i == 1:
                        wait_self("m0")
                    dvs.done(nc.vector.tensor_scalar(T[1][:, 0:SEQ], psX[:, 2 + i, :], cols[:, gcol:gcol + 1], None,
                                                     ALU.mult), f"og{i}")
                    wait_self(f"og{i}")
                    wait_act(f"rinv{i}")
                    dvs.done(nc.vector.tensor_tensor(T[1][:, 0:SEQ], T[1][:, 0:SEQ], T[3][:, 0:SEQ], ALU.mult),
                             f"on{i}")
                    wait_self(f"on{i}")
                    dst = mT[:, 2 * n + i:2 * n + i + 1, :] if kind == "G" else mT[:, bass.ds(n + 4, 1), :]
                    dvs.done(nc.vector.tensor_tensor(dst, T[1][:, 0:SEQ].unsqueeze(1), gates[i][:, :].unsqueeze(1),
                                                     ALU.mult), f"m{i}")
                dvs.end()

            for pr in range(GLA_PAIRS):
                mixer(("G", pr))
            with dve.Fori(0, HGRN_HEADS) as h:
                mixer(("H", h))
            for k in range(KT):
                dve.wait_ge(s_mhi, k + 1)
                nc.vector.tensor_tensor(h_lo[:, k, TC * P:TOK], mT[:, k, :],
                                        h_hi[:, k, TC * P:TOK].bitcast(F32), ALU.subtract).then_inc(s_m, 1)
            gate_of(1)
            scale_of(2)
            for i in range(2):
                for s in range(2):
                    split_lo(s, mix_out_pair + i + 1)
            for q in range(TT, TT + TL):
                post(q)
                pre(TT + q)
            ffn(ffn_phases["F"], ffn2, n2, lambda p: False)
            gate_of(2)
            for q in range(TT + TL, TT + 2 * TL):
                post(q)

        @block.tensor
        def _(pe):
            def product(dst, w_h, w_l, x_h, x_l, start, stop):
                nc.tensor.matmul(dst, w_l, x_h, start=start, stop=False)
                nc.tensor.matmul(dst, w_h, x_l, start=False, stop=False)
                return nc.tensor.matmul(dst, w_h, x_h, start=False, stop=stop)

            def project(s, view, c, width, cells):
                for dst, a, n in cells:
                    for k in range(KT):
                        ins = product(dst, view(w_hi[s])[:, k, c:c + width], view(w_lo[s])[:, k, c:c + width],
                                      h_hi[:, k, a:a + n], h_lo[:, k, a:a + n], k == 0, k == KT - 1)
                return ins

            def ada(b):
                pe.wait_ge(s_ada_loaded, b * 16 + 16)
                pe.wait_ge(s_ada_out, b)
                for j in range(2):
                    for k in range(KT):
                        ins = nc.tensor.matmul(ada_ps[:, j, :], w_ada[:, k, j * P:(j + 1) * P],
                                               small[:, k:16:KT], start=k == 0, stop=k == KT - 1)
                ins.then_inc(s_ada_done, 1)

            def pre(q):
                pe.wait_ge(s_xn, q + 1)
                pe.wait_ge(s_mod, q)
                pe.wait_ge(s_r, 0 if q < TT else q - TT + 1)
                for k in range(KT):
                    ins = nc.tensor.transpose(turn[:, k * P:(k + 1) * P], xn[:, k * P:(k + 1) * P], ident[:, :])
                ins.then_inc(s_turned, 1)

            def post(q, yT, c0):
                pe.wait_ge(s_mod, q + TT if q < TT + TL else 2 * TT + TL)
                pe.wait_ge(s_r, q)
                for k in range(KT):
                    ins = nc.tensor.transpose(turn[:, k * P:(k + 1) * P], yT[:, k, c0:c0 + P], ident[:, :])
                ins.then_inc(s_yturned, 1)

            def ffn(phases, bufs, n, c0, with_ada):
                hid_hi, hid_lo, yT, _, _ = bufs
                view = lambda w: slot_view(w, KT, 256)
                for j, (tiles, _, p_in, p_out, i0, _) in enumerate(phases):
                    if j:
                        pe.wait_ge(s_y0, y0_after[p_in] + SEED)
                        pe.wait_ge(s_y1, y1_before[p_in] + SEED)
                    with pe.Fori(0, tiles // 2) as i:
                        p = i + p_in
                        for s, free in ((0, s_silu), (1, s_hf)):
                            pe.wait_ge(s_lo[s], p + 1 + SEED)
                            pe.wait_ge(free, i * 2 + 2 * i0 + SEED)
                            for u in range(2):
                                ins = project(s, view, u * P, P, [(psA[:, 2 * s + u, 0:n], c0, n)])
                            ins.then_inc(s_done[s], 1)
                        if with_ada(p_in):
                            ada(p + ADA_FIRST)
                    pe.wait_ge(s_hid, 2 * i0 + tiles + SEED)

                    def out_pair(p, u):
                        kk = tiles // 2
                        for s in range(2):
                            pe.wait_ge(s_lo[s], p + 1 + SEED)
                            for v in range(2):
                                for k in range(kk):
                                    hk = s * kk + k
                                    c = slice(v * P, (v + 1) * P)
                                    ins = product(psA[:, 2 * u + v, 0:n], slot_view(w_hi[s], kk, 256)[:, k, c],
                                                  slot_view(w_lo[s], kk, 256)[:, k, c], hid_hi[:, hk, :],
                                                  hid_lo[:, hk, :], hk == 0, hk == tiles - 1)
                            ins.then_inc(s_done[s], 1)

                    with pe.Fori(0, 2) as hh:
                        for u in range(2):
                            p = hh * 2 + (p_out + u)
                            if j == 0:
                                pe.wait_ge(s_y0, hh * 4 + y0_wait[p_out][u] + SEED)
                            else:
                                pe.wait_ge(s_y1, hh * 4 + y1_wait[p_out][u] + SEED)
                            out_pair(p, u)
                            if with_ada(p_out):
                                ada(p + ADA_FIRST)

            pe.wait_ge(s_const, 16 * 13)
            nc.tensor.transpose(psX[:, 3, 0:N_ROWS], rows[0:N_ROWS, :], ident[0:N_ROWS, 0:N_ROWS]).then_inc(s_cols_ps, 1)
            pe.wait_ge(s_silu_c, 1)
            for b in range(ADA_FIRST):
                ada(b)
            for q in range(TT):
                pre(q)
            pe.wait_ge(s_h, TT)
            for g, (t0, nt) in enumerate(FFN1_GROUPS):
                ffn(ffn_phases["AB"[g]], ffn1, n1, t0 * P,
                    (lambda p: True) if g == 0 else (lambda p: p + ADA_FIRST < ADA_BLOCKS))
                pe.wait_ge(s_ygate, g + 1)
                for q in range(t0, t0 + nt):
                    post(q, ffn1[2], (q - t0) * P)
                    pre(TT + q)

            def mixer(g):
                kind, n = g
                pes.start(g)
                p = mix_group_pair(g)
                heads = heads_of(kind)

                def wait_act(name):
                    pe.wait_ge(acs.sem, acs.at(g, name))

                def wait_dve(name):
                    pe.wait_ge(dvs.sem, dvs.at(g, name))

                def all_tokens(bank):
                    return [(psA[:, bank, 0:n1], 0, n1), (psA[:, bank + 1, 0:n1], n1, n1)]

                pe.wait_ge(acs.sem, acs.before(g))
                pe.wait_ge(dvs.sem, dvs.before(g))
                one = lambda w: slot_view(w, KT, P)
                second = lambda w: slot_view(w, 2 * KT, P)[:, KT:2 * KT, :]
                wide = lambda w: slot_view(w, KT, 256)
                x_all = [(psX[:, 0, 0:n1], 0, n1), (psX[:, 1, 0:n1], n1, n1)]
                pe.wait_ge(s_lo[0], p + 1 + SEED)
                if kind == "H":
                    project(0, one, 0, P, all_tokens(0)).then_inc(s_done[0], 1)
                    pe.wait_ge(s_lo[1], p + 1 + SEED)
                    project(1, one, 0, P, all_tokens(2)).then_inc(s_done[1], 1)
                    pe.wait_ge(s_lo[0], p + 2 + SEED)
                    project(0, one, 0, P, x_all).then_inc(s_done[0], 1)
                    pe.wait_ge(s_lo[1], p + 2 + SEED)
                    project(1, one, 0, P, [(psX[:, 2, :], TC * P, SEQ)])
                    project(1, second, 0, P, [(psX[:, 3, :], TC * P, SEQ)]).then_inc(s_done[1], 1)
                else:
                    ins = project(0, one, 0, P, all_tokens(0))
                    if n == 0:
                        ins = project(0, second, 0, P, [(psA[:, 2, :], TC * P, SEQ)])
                    ins.then_inc(s_done[0], 1)
                    pe.wait_ge(s_lo[1], p + 1 + SEED)
                    if n == 0:
                        low = lambda w: slot_view(w, KT, 32)
                        ins = project(1, low, 0, 32, [(psX[0:32, i, 0:n1], i * n1, n1) for i in range(2)])
                    else:
                        ins = project(1, one, 0, P, [(psA[:, 2, :], TC * P, SEQ)])
                    ins.then_inc(s_done[1], 1)
                    pe.wait_ge(s_lr, 1)
                    pe.wait_ge(s_a2, 32)
                    for d in range(2):
                        for i in range(2):
                            ins = nc.tensor.matmul(psX[:, 2 * d + i, 0:n1], a2[d][:, n * P:(n + 1) * P],
                                                   lr[:, i * n1:(i + 1) * n1], start=True, stop=True)
                        pes.done(ins, f"z{d}")
                    wait_act("q")
                    pe.wait_ge(s_lo[0], p + 2 + SEED)
                    for i in range(2):
                        ins = project(0, wide, i * P, P, all_tokens(2 * i))
                    ins.then_inc(s_done[0], 1)
                    wait_act("z1")
                    pe.wait_ge(s_lo[1], p + 2 + SEED)
                    for i in range(2):
                        ins = project(1, wide, i * P, P, [(psX[:, 2 + i, :], TC * P, SEQ)])
                    ins.then_inc(s_done[1], 1)
                for i, _, _ in heads:
                    wait_act(f"vf{i}")
                    if i == 1:
                        wait_act("vt0b")
                    for tt in range(TT):
                        dst = psX[:, tt // 4, (tt % 4) * P:(tt % 4 + 1) * P]
                        ins = nc.tensor.transpose(dst, vf[:, tt * P:(tt + 1) * P], ident[:, :])
                    pes.done(ins, f"vT{i}")
                wait_act(f"vt{heads[-1][0]}b")

                def turn_tail(m):
                    s, d = m // 2, m % 2
                    if s == 0:
                        wait_dve(f"tail{d}")
                    else:
                        wait_dve(f"kt{m - 2}")
                    tt = scan_tiles(d)[s]
                    pes.done(nc.tensor.transpose(psX[:, d, 0:P], tail[d][:, tt * P:(tt + 1) * P], ident[:, :]),
                             f"T{m}")

                turn_tail(0)
                for m in range(2 * TT):
                    if m + 1 < 2 * TT:
                        turn_tail(m + 1)
                    s, d = m // 2, m % 2
                    tt = scan_tiles(d)[s]
                    wait_dve(f"kt{m}")
                    if s:
                        wait_dve(f"S{d}_{s * CPT - 1}")
                    for c in range(CPT):
                        for i, p0, pn in heads:
                            ins = nc.tensor.matmul(psA[p0:p0 + pn, d, c * P:(c + 1) * P],
                                                   kt4[d][:, c, p0:p0 + pn], vtok[i][:, tt, :],
                                                   start=True, stop=True, skip_group_check=True)
                    pes.done(ins, f"U{m}")
                wait_dve("qdec1")
                for d in range(2):
                    wait_dve(f"S{d}_{NCH - 2}")
                seq = [(a, i) for a in range(TL) for i, _, _ in heads]
                for at, (tt, i) in enumerate(seq):
                    _, p0, pn = heads[i]
                    cols_t = slice(tt * P, (tt + 1) * P)
                    for d in range(2):
                        if at:
                            wait_dve(f"am{seq[at - 1][0]}{seq[at - 1][1]}{d}")
                        pes.done(nc.tensor.matmul(psA[:, 2 + d, 0:P], kinv[d][p0:p0 + pn, cols_t],
                                                  qdec[d][p0:p0 + pn, cols_t], start=True, stop=True), f"att{tt}{i}{d}")
                    o = psX[:, 2 + i, :]
                    for d in range(2):
                        wait_dve(f"am{tt}{i}{d}")
                        ins = nc.tensor.matmul(o[:, cols_t], vtok[i][:, TC + tt, :], attT[:, d, :],
                                               start=d == 0, stop=False, skip_group_check=True)
                        if d == 0:
                            pes.done(ins, f"intra{tt}{i}0")
                    for d in range(2):
                        for c in range(CPT):
                            ch = tt * CPT + c
                            m = ch if d == 0 else LC - 1 - ch
                            cc = slice(ch * CHUNK, (ch + 1) * CHUNK)
                            ins = nc.tensor.matmul(o[:, cc], St[d][p0:p0 + pn, m, :], qdec[d][p0:p0 + pn, cc],
                                                   start=False, stop=True, skip_group_check=True)
                    pes.done(ins, f"o{tt}{i}")
                for i, _, _ in heads:
                    wait_act(f"sq{i}")
                    pes.done(nc.tensor.matmul(psA[:, i, :], ones[:, :], T[0][:, 0:SEQ], start=True, stop=True),
                             f"ms{i}")
                pes.end()

            pe.wait_ge(s_h, 2 * TT)
            for pr in range(GLA_PAIRS):
                mixer(("G", pr))
            with pe.Fori(0, HGRN_HEADS) as h:
                mixer(("H", h))
            pe.wait_ge(s_m, KT)
            pe.wait_ge(acs.sem, acs.before(("H", HGRN_HEADS)))
            for i in range(2):
                for s in range(2):
                    pe.wait_ge(s_lo[s], mix_out_pair + i + 1 + SEED)
                    if i:
                        pe.wait_ge(s_mo, 2 * s + 2)
                    for u in range(2):
                        ins = project(s, lambda w: slot_view(w, KT, 256), u * P, P,
                                      [(psA[:, 2 * s + u, :], TC * P, SEQ)])
                    ins.then_inc(s_done[s], 1)
            pe.wait_ge(s_mo, KT)
            for q in range(TT, TT + TL):
                post(q, mT, (q - TT) * P)
                pre(TT + q)
            pe.wait_ge(s_h, len(pre_jobs))
            ffn(ffn_phases["F"], ffn2, n2, TC * P, lambda p: False)
            pe.wait_ge(s_ygate, 3)
            for q in range(TT + TL, TT + 2 * TL):
                post(q, ffn2[2], (q - TT - TL) * P)


def position_rows():
    import numpy as np

    quarter = D // 4
    omega = np.float32(1.0) / np.power(np.float32(10000.0), np.arange(quarter, dtype=np.float32) / np.float32(quarter))

    def emb(n):
        a = np.arange(n).astype(np.float32)[:, None] * omega.astype(np.float32)[None, :]
        return np.concatenate([np.sin(a), np.cos(a)], axis=-1).astype(np.float32)

    return emb(SEQ // 64), np.tile(emb(64), (2, 1))


def constants():
    import numpy as np

    j, i = np.meshgrid(np.arange(P), np.arange(P), indexing="ij")
    same = j // CHUNK == i // CHUNK
    prow, pcol = position_rows()
    starts = np.where(np.arange(TOK) % CHUNK == 0, 0.0, 1.0)
    return {
        "k_ident": np.eye(P, dtype=np.float32),
        "k_ones": np.ones((P, P), np.float32),
        "k_cmask": (j[:, 0:1] // CHUNK == np.arange(CPT)[None, :]).astype(np.float32),
        "k_smask": np.tile(starts[None, :], (P, 1)).astype(mybir.dt.np(mybir.dt.bfloat16)),
        "k_amask": np.stack([same & (j <= i), same & (j >= i)], axis=1).astype(np.int32),
        "k_prow": prow,
        "k_pcol": pcol,
    }


def kernel(**inputs):
    import numpy as np
    import concourse.bacc as bacc
    from concourse.bass_utils import run_bass_kernel_spmd as run

    shapes = {
        "x": (SEQ, D), "ctx": (CTX, D), "c": (8, P), "c_ctx": (8, P), "w_ada": (D, 9 * D), "b_ada": (72, P),
        "ln_gain": (3, D), "ln_bias": (3, D), "ffn1_w_in": (D, 2 * FF), "ffn1_w_out": (FF, D),
        "w_mix_in": (D, 4128), "gla_a2_fwd": (16, 256), "gla_a2_bwd": (16, 256), "gla_a_bias_fwd": (2, P),
        "gla_a_bias_bwd": (2, P), "hgrn_lb_logits": (16, P), "gla_norm_gain": (1, P), "hgrn_norm_gain": (1, P),
        "w_mix_out": (D, D), "ffn2_w_in": (D, 2 * FF), "ffn2_w_out": (FF, D),
    }
    arrays = {n: np.ascontiguousarray(inputs[n]).reshape(s) for n, s in shapes.items()}
    arrays.update(constants())
    nc = bacc.Bacc("TRN2", target_bir_lowering=False, num_devices=1)
    tensors = {n: nc.dram_tensor(n, a.shape, mybir.dt.from_np(a.dtype), kind="ExternalInput").ap()
               for n, a in arrays.items()}
    out = nc.dram_tensor("out", (SEQ, D), F32, kind="ExternalOutput").ap()
    build(nc, tensors, out)
    result = run(nc, [arrays], core_ids=[0])
    return result.results[0]["out"].reshape(1, SEQ, D)
```

```python
from contextlib import ExitStack

import concourse.bass as bass
from concourse import mybir

F32 = mybir.dt.float32
F32R = mybir.dt.float32r
I32 = mybir.dt.int32
ALU = mybir.AluOpType
ACT = mybir.ActivationFunctionType

P = 128
D = 1024
KT = D // P
FF = 2816
CTX, SEQ = 256, 512
TOK = CTX + SEQ
TC, TL = CTX // P, SEQ // P
TT = TC + TL
CHUNK = 32
NCH = TOK // CHUNK
CPT = P // CHUNK
CC = CTX // CHUNK
LC = SEQ // CHUNK
ALPHA = 2.0 ** 0.25
GLA_PAIRS, HGRN_HEADS = 2, 4
C_GQ, C_GK, C_GV, C_GG, C_LR = 0, 256, 512, 1024, 1536
C_RQ, C_RFF, C_RFB, C_RI, C_RG = 1568, 2080, 2592, 3104, 3616
R_BADA, R_GBIAS, R_LB, R_GAIN, R_C = 0, 72, 76, 92, 94
N_ROWS = 110
SLOT = 8 * 256

FFN1_GROUPS = ((0, 3), (3, 3))
FFN1_PARTS = (12, 10)
FFN2_PARTS = (8, 8, 6)
ADA_FIRST = 8
ADA_BLOCKS = 36
SEED = 1


class Steps:

    def __init__(self, sem, names_gla, names_hgrn):
        self.sem, self.names = sem, {"G": list(names_gla), "H": list(names_hgrn)}
        self.turn = 0

    def at(self, group, name):
        kind, n = group
        base = 0 if kind == "G" else GLA_PAIRS * len(self.names["G"])
        return base + n * len(self.names[kind]) + (self.names[kind].index(name) + 1)

    def before(self, group):
        kind, n = group
        base = 0 if kind == "G" else GLA_PAIRS * len(self.names["G"])
        return base + n * len(self.names[kind])

    def start(self, group):
        self.kind, self.turn = group[0], 0

    def done(self, ins, name):
        assert self.names[self.kind][self.turn] == name, (self.names[self.kind][self.turn], name)
        self.turn += 1
        ins.then_inc(self.sem, 1)

    def end(self):
        assert self.turn == len(self.names[self.kind])


def heads_of(kind):
    return ((0, 0, 64), (1, 64, 64)) if kind == "G" else ((0, 0, 128),)


def scan_tiles(d):
    return list(range(TT)) if d == 0 else list(range(TC))[::-1] + list(range(TC, TT))[::-1]


def pe_names(kind):
    out = ["z0", "z1"] if kind == "G" else []
    out += [f"vT{i}" for i, _, _ in heads_of(kind)]
    out[-1:] = ["T0", "T1", out[-1]]
    for n in range(2 * TT):
        if 1 <= n < 2 * TT - 1:
            out.append(f"T{n + 1}")
        out.append(f"U{n}")
    seq = [f"{t}{i}" for t in range(TL) for i, _, _ in heads_of(kind)]
    out += [f"att{seq[0]}0", f"att{seq[0]}1"]
    for at, job in enumerate(seq):
        if at + 1 < len(seq):
            out += [f"att{seq[at + 1]}0", f"att{seq[at + 1]}1"]
        out.append(f"o{job}")
    out += [f"ms{i}" for i, _, _ in heads_of(kind)]
    return out


def act_names(kind):
    gating = lambda d: [f"eb{d}", f"einv{d}", f"dec{d}", f"tail{d}"]
    if kind == "H":
        out = ["sig0", "sig1", "ln0"] + gating(0) + ["ln1"] + gating(1)
        out += ["vf0", "vt0a", "vt0b", "sigq", "sigg0"]
    else:
        out = ["k", "q", "z0", "z1"]
        for d in range(2):
            out += [f"abs{d}", f"ex{d}", f"ln{d}"] + gating(d)
        out += ["vf0", "vt0a", "vt0b", "vf1", "vt1a", "vt1b", "sigg0", "sigg1"]
    out += [x for i, _, _ in heads_of(kind) for x in (f"sq{i}", f"lnms{i}", f"rinv{i}")]
    return out


def dve_names(kind):
    out = ["lb"] if kind == "H" else []
    for d in range(2):
        out += [f"f{d}", f"k{d}"] if kind == "H" else [f"zm{d}", f"g{d}"]
        out += [f"b{d}", f"diff{d}", f"kinv{d}", f"tail{d}"]
    out += ["kt0", "kt1"]
    for s in range(TT):
        if s + 1 < TT:
            out += [f"kt{2 * s + 2}", f"kt{2 * s + 3}"]
        for c in range(CPT):
            for d in range(2):
                if s * CPT + c < NCH - 1:
                    out.append(f"S{d}_{s * CPT + c}")
        if s == 0:
            out += ["q", "gate0"] if kind == "H" else ["gate0", "gate1"]
        elif s <= 2:
            out.append(f"qdec{s - 1}")
    for t in range(TL):
        for i, _, _ in heads_of(kind):
            out += [f"am{t}{i}0", f"am{t}{i}1"]
    out += [x for i, _, _ in heads_of(kind) for x in (f"og{i}", f"on{i}", f"m{i}")]
    return out


def build(nc, t, out):
    with ExitStack() as ctx:
        def sb(name, shape, dt=F32, where=ctx):
            return where.enter_context(nc.sbuf_tensor(name, shape, dt))

        def sem(name):
            return ctx.enter_context(nc.semaphore(name))

        h_hi = sb("h_hi", [P, KT, TOK], F32R)
        h_lo = sb("h_lo", [P, KT, TOK], F32R)
        xtok = sb("xtok", [P, TT, D])
        w_raw = [sb(f"w_raw{s}", [P, SLOT]) for s in range(2)]
        w_hi = [sb(f"w_hi{s}", [P, SLOT], F32R) for s in range(2)]
        w_lo = [sb(f"w_lo{s}", [P, SLOT], F32R) for s in range(2)]
        work = sb("work", [P, 4 * D])
        gain_b, bias_b, xn = (work[:, i * D:(i + 1) * D] for i in range(3))
        hfull = work[:, 3 * D:4 * D].rearrange("p (k c) -> p k c", c=P)
        ident = sb("ident", [P, P])
        ones = sb("ones", [P, P])
        rows = sb("rows", [P, P])
        cols = sb("cols", [P, N_ROWS])
        mods = sb("mods", [P, 72, 2])
        scale1 = sb("scale1", [P, KT, 2])
        gate_w = sb("gate_w", [P, KT, 2])
        lb = sb("lb", [P, 2, HGRN_HEADS])
        lb1 = sb("lb1", [P, 2, HGRN_HEADS])
        small = sb("small", [P, 32])
        stats = sb("stats", [P, 12])
        mv = sb("mv", [P, 2])
        std = sb("std", [P, 1])
        rstd = sb("rstd", [P, 1])
        eps_ln = sb("eps_ln", [P, 1])
        eps_rms = sb("eps_rms", [P, 1])
        cmask = sb("cmask", [P, CPT])
        smask = sb("smask", [P, TOK], mybir.dt.bfloat16)
        amask = sb("amask", [P, 2, P], I32)
        attT = [sb(f"attT{i}", [P, 2, P]) for i in range(2)]

        def ffn_set(where, tag, n_hidden, n):
            return (sb(f"hid_hi_{tag}", [P, n_hidden, n], F32R, where),
                    sb(f"hid_lo_{tag}", [P, n_hidden, n], F32R, where),
                    sb(f"yT_{tag}", [P, KT, n], F32, where),
                    sb(f"glu_{tag}", [P, 4, n], F32, where))

        n1, n2 = FFN1_GROUPS[0][1] * P, SEQ
        with ExitStack() as s1:
            ffn1 = ffn_set(s1, "ffn1", max(FFN1_PARTS), n1)
            ada_slots = [sb("ada_block", [P, KT, 256], F32, s1)]
            ada_row = sb("ada_row", [2, 256], F32, s1)
        with ExitStack() as s0:
            ada_slots += [sb(f"ada_block{i}", [P, KT, 256], F32, s0) for i in range(1, 4)]
        with ExitStack() as s2:
            mT = sb("mT", [P, KT, SEQ], F32, s2)
            St = [sb(f"state{d}", [P, LC, P], F32, s2) for d in range(2)]
            qdec = [sb(f"qdec{d}", [P, SEQ], F32, s2) for d in range(2)]
            kinv = [sb(f"kinv{d}", [P, SEQ], F32, s2) for d in range(2)]
            tail = [sb(f"tail{d}", [P, TOK], F32, s2) for d in range(2)]
            vtok = [sb(f"vtok{i}", [P, TT, P], F32, s2) for i in range(2)]
            qf = sb("qf", [P, SEQ], F32, s2)
            gates = [sb(f"gate{i}", [P, SEQ], F32, s2) for i in range(2)]
            dec = [sb(f"dec{d}", [P, NCH], F32, s2) for d in range(2)]
            kt4 = [sb(f"kt4_{i}", [P, CPT, P], F32, s2) for i in range(2)]
            lbh = sb("lbh", [P, 2, 2], F32, s2)
        with ExitStack() as s3:
            ffn2 = ffn_set(s3, "ffn2", max(FFN2_PARTS), n2)
        T = [work[:, i * TOK:(i + 1) * TOK] for i in range(5)]
        ctx_part = xtok[:, 0:TC, :].rearrange("p a b -> p (a b)")
        lr = ctx_part[0:32, 0:TOK]
        a2 = [ctx_part[0:32, TOK + d * 256:TOK + (d + 1) * 256] for d in range(2)]
        vf = ctx_part[:, TOK + 512:2 * TOK + 512]
        yT1 = ffn1[2][:, :, :].rearrange("p k c -> p (k c)")
        prow = [yT1[:, i * 512:(i + 1) * 512] for i in range(TL)]
        pcol = yT1[:, TL * 512:(TL + 1) * 512]

        psA = ctx.enter_context(nc.psum_tensor("psA", [P, 4, 512], F32))
        psX = ctx.enter_context(nc.psum_tensor("psX", [P, 4, 512], F32))
        turn = psX[:, 0:2, :].rearrange("p a b -> p (a b)")
        turn_y = psX[:, 2:4, :].rearrange("p a b -> p (a b)")
        ada_row_ps = psX[0:2, 3, 0:256]
        ada_ps = psX[:, 2, 0:4].rearrange("p (a b) -> p a b", b=2)

        def tail_ps(m):
            return (psA[:, 2 + m, 0:P] if m < 2 else psX[:, m % 2, 0:P])

        def ada_slot(b):
            return ada_slots[0 if b is None else b % 4]

        def xn_of(q):
            glu = ffn1[3] if q < 2 * TT else ffn2[3]
            return xn if q % 2 == 0 else glu[:, :, :].rearrange("p a b -> p (a b)")[:, 0:D]

        s_zero = sem("constants_set")
        s_const = sem("constants_loaded")
        s_x = sem("x_loaded")
        s_loaded = [sem(f"slot{s}_loaded") for s in range(2)]
        s_hi = [sem(f"slot{s}_hi_ready") for s in range(2)]
        s_lo = [sem(f"slot{s}_lo_ready") for s in range(2)]
        s_done = [sem(f"slot{s}_products_done") for s in range(2)]
        s_ada_first = [sem(f"ada_slot{i}_loaded") for i in range(4)]
        s_ada_loaded = sem("ada_loaded")
        s_ada_done = sem("ada_products_done")
        s_ada_out = sem("ada_evacuated")
        s_ada_row = sem("ada_rows_taken")
        s_ada_turned = sem("ada_rows_turned")
        s_cols_ps = sem("cols_turned")
        s_cols = sem("cols_ready")
        s_silu_c = sem("silu_c_ready")
        s_lbe = sem("lb_exp_ready")
        s_own = sem("vector_chain")
        s_scale = sem("scale_ready")
        s_stat = sem("stats_ready")
        s_std = sem("std_ready")
        s_xn = sem("xn_ready")
        s_turned = sem("x_turned")
        s_mod = sem("modulated")
        s_hhi = sem("h_hi_ready")
        s_h = sem("h_ready")
        s_ygate = sem("y_gated")
        s_yturned = sem("y_turned")
        s_r = sem("residual_summed")
        s_xnew = sem("x_updated")
        s_silu = sem("silu_ready")
        s_hf = sem("hidden_ready")
        s_hidhi = sem("hidden_hi_ready")
        s_hid = sem("hidden_split")
        s_y0 = sem("y_first_part")
        s_y1 = sem("y_later_part")
        s_gb = sem("gain_bias_loaded")
        s_a2 = sem("a2_loaded")
        s_a2z = sem("a2_zeroed")
        s_lr = sem("lr_ready")
        s_mask_turn = sem("mask_turns")
        s_mhi = sem("merged_hi_ready")
        s_m = sem("merged_split")
        s_mo = sem("mixer_out_evacuated")
        s_out = sem("output_stored")
        pes = Steps(sem("mixer_tensor_step"), pe_names("G"), pe_names("H"))
        acs = Steps(sem("mixer_scalar_step"), act_names("G"), act_names("H"))
        dvs = Steps(sem("mixer_vector_step"), dve_names("G"), dve_names("H"))

        ffn_phases = {}
        pair, n_in, n_out = 0, 0, 0
        for name, parts in (("A", FFN1_PARTS), ("B", FFN1_PARTS), ("mix", None), ("F", FFN2_PARTS)):
            if parts is None:
                mix_pair = pair
                mix_out_pair = pair + 2 * (GLA_PAIRS + HGRN_HEADS)
                pair = mix_out_pair + 2
                continue
            first, ph = 0, []
            for n in parts:
                ph.append((n, first, pair, pair + n // 2, n_in, n_out))
                pair += n // 2 + 4
                n_in += n // 2
                n_out += 4
                first += n
            ffn_phases[name] = ph
        last_pair = pair - 1
        ada_plan, ada_after, block_at = {}, [], ADA_FIRST
        for name in "AB":
            for n, _, p_in, p_out, _, _ in ffn_phases[name]:
                for start, count in ((p_in, n // 2), (p_out, 4)):
                    if block_at + count > ADA_BLOCKS:
                        continue
                    extra = (ADA_BLOCKS - ADA_FIRST) - 25 > len(ada_plan)
                    ada_plan[start] = (block_at - start, block_at + count if extra else None)
                    block_at += count + extra
            ada_after.append(block_at)
        assert block_at == ADA_BLOCKS
        y0_before, y1_before, y0_after, y1_after, y0_wait, y1_wait = {}, {}, {}, {}, {}, {}
        n0 = n_1 = 0
        for name in ("A", "B", "F"):
            ph = ffn_phases[name]
            for j, (_, _, p_in, p_out, _, _) in enumerate(ph):
                y0_after[p_in] = y0_after[p_out] = n0
                y1_before[p_in] = y1_before[p_out] = n_1
                y0_wait[p_out] = [max(n0 - 2 + 2 * u, 0) if j == 0 else n0 for u in range(2)]
                y1_wait[p_out] = [max(n_1 - 2 + 2 * u, 0) if j else n_1 for u in range(2)]
                y0_wait[p_out][0] = max(n0 - 2, 0)
                y1_wait[p_out][0] = max(n_1 - 2, 0)
                if j == 0:
                    n0 += KT
                else:
                    n_1 += KT
            y1_after[ph[0][2]] = n_1
        pre_jobs = ([(tt, 0) for tt in range(TT)] + [(tt, 1) for tt in range(TT)]
                    + [(tt, 2) for tt in range(TC, TT)])
        post_jobs = [(tt, 0) for tt in range(TT)] + [(tt, s) for s in (1, 2) for tt in range(TC, TT)]

        w1i = t["ffn1_w_in"].rearrange("(k p) n -> p k n", p=P)
        w1o = t["ffn1_w_out"].rearrange("(k p) n -> p k n", p=P)
        w2i = t["ffn2_w_in"].rearrange("(k p) n -> p k n", p=P)
        w2o = t["ffn2_w_out"].rearrange("(k p) n -> p k n", p=P)
        wmi = t["w_mix_in"].rearrange("(k p) n -> p k n", p=P)
        wmo = t["w_mix_out"].rearrange("(k p) n -> p k n", p=P)
        wad = t["w_ada"].rearrange("(k p) n -> p k n", p=P)

        def slot_view(buf, k, c):
            return buf[:, 0:k * c].rearrange("p (k c) -> p k c", c=c)

        def halves(k):
            return (0, (k + 1) // 2), ((k + 1) // 2, k)

        def mix_group_pair(g):
            return mix_pair + 2 * g[1] + (2 * GLA_PAIRS if g[0] == "H" else 0)

        block = ctx.enter_context(nc.Block())

        @block.sync
        def _(sp):
            def slot_free(s, p):
                sp.wait_ge(s_lo[s], p + SEED)

            def ffn_loads(phases, wi, wo):
                for n, first, p_in, p_out, _, _ in phases:
                    with sp.Fori(p_in, p_in + n // 2) as p:
                        for s in range(2):
                            slot_free(s, p)
                            c0 = (first - 2 * p_in) * P + s * FF
                            for a, b in halves(KT):
                                sp.dma_start(slot_view(w_raw[s], KT, 256)[:, a:b, :],
                                             wi[:, a:b, bass.ds(p * 256 + c0, 256)]).then_inc(s_loaded[s], 16)
                    with sp.Fori(p_out, p_out + 4) as p:
                        for s in range(2):
                            slot_free(s, p)
                            k0 = first + s * (n // 2)
                            for a, b in halves(n // 2):
                                sp.dma_start(slot_view(w_raw[s], n // 2, 256)[:, a:b, :],
                                             wo[:, k0 + a:k0 + b, bass.ds(p * 256 - p_out * 256, 256)]
                                             ).then_inc(s_loaded[s], 16)

            def gain_bias(s):
                for dst, name in ((gain_b, "ln_gain"), (bias_b, "ln_bias")):
                    sp.dma_start(dst, t[name][s:s + 1, :].broadcast_to([P, D])).then_inc(s_gb, 16)

            sp.dma_start(rows[R_BADA:R_BADA + 72, :], t["b_ada"]).then_inc(s_const, 16)
            sp.dma_start(rows[R_GBIAS:R_GBIAS + 2, :], t["gla_a_bias_fwd"]).then_inc(s_const, 16)
            sp.dma_start(rows[R_GBIAS + 2:R_GBIAS + 4, :], t["gla_a_bias_bwd"]).then_inc(s_const, 16)
            sp.dma_start(rows[R_LB:R_LB + 16, :], t["hgrn_lb_logits"]).then_inc(s_const, 16)
            sp.dma_start(rows[R_GAIN:R_GAIN + 1, :], t["gla_norm_gain"]).then_inc(s_const, 16)
            sp.dma_start(rows[R_GAIN + 1:R_GAIN + 2, :], t["hgrn_norm_gain"]).then_inc(s_const, 16)
            sp.dma_start(rows[R_C:R_C + 8, :], t["c"]).then_inc(s_const, 16)
            sp.dma_start(rows[R_C + 8:R_C + 16, :], t["c_ctx"]).then_inc(s_const, 16)
            sp.dma_start(ident[:, :], t["k_ident"]).then_inc(s_const, 16)
            sp.dma_start(ones[:, :], t["k_ones"]).then_inc(s_const, 16)
            sp.dma_start(cmask[:, :], t["k_cmask"]).then_inc(s_const, 16)
            sp.dma_start(smask[:, :], t["k_smask"]).then_inc(s_const, 16)
            sp.dma_start(amask[:, :, :], t["k_amask"]).then_inc(s_const, 16)
            for tt in range(TC):
                sp.dma_start(xtok[:, tt, :], t["ctx"][tt * P:(tt + 1) * P, :]).then_inc(s_x, 16)
            for i in range(TL):
                sp.dma_start(xtok[:, TC + i, :], t["x"][i * P:(i + 1) * P, :]).then_inc(s_x, 16)
                for r in range(2):
                    sp.dma_start(prow[i][r * 64:(r + 1) * 64, :],
                                 t["k_prow"][2 * i + r:2 * i + r + 1, :].broadcast_to([64, 512])).then_inc(s_x, 16)
            sp.dma_start(pcol, t["k_pcol"]).then_inc(s_x, 16)
            gain_bias(0)
            ffn_loads(ffn_phases["A"], w1i, w1o)
            ffn_loads(ffn_phases["B"], w1i, w1o)

            def mix_slot(s, p, *pieces):
                slot_free(s, p)
                if len(pieces) == 2:
                    for i, c0 in enumerate(pieces):
                        sp.dma_start(slot_view(w_raw[s], 2 * KT, P)[:, i * KT:(i + 1) * KT, :],
                                     wmi[:, :, bass.ds(c0, P)]).then_inc(s_loaded[s], 16)
                    return
                (c0, width), = pieces
                for a, b in halves(KT):
                    sp.dma_start(slot_view(w_raw[s], KT, width)[:, a:b, :],
                                 wmi[:, a:b, bass.ds(c0, width)]).then_inc(s_loaded[s], 16)

            for pr in range(GLA_PAIRS):
                p = mix_group_pair(("G", pr))
                if pr == 0:
                    mix_slot(0, p, C_GK, C_GQ)
                    mix_slot(1, p, (C_LR, 32))
                else:
                    mix_slot(0, p, (C_GK + P * pr, P))
                    mix_slot(1, p, (C_GQ + P * pr, P))
                mix_slot(0, p + 1, (C_GV + 2 * P * pr, 2 * P))
                mix_slot(1, p + 1, (C_GG + 2 * P * pr, 2 * P))
            with sp.Fori(0, HGRN_HEADS) as h:
                p = mix_group_pair(("H", h))
                mix_slot(0, p, (h * P + C_RFF, P))
                mix_slot(1, p, (h * P + C_RFB, P))
                mix_slot(0, p + 1, (h * P + C_RI, P))
                mix_slot(1, p + 1, h * P + C_RQ, h * P + C_RG)
            for i in range(2):
                p = mix_out_pair + i
                for s in range(2):
                    slot_free(s, p)
                    for a, b in halves(KT):
                        sp.dma_start(slot_view(w_raw[s], KT, 256)[:, a:b, :],
                                     wmo[:, a:b, (2 * i + s) * 256:(2 * i + s + 1) * 256]).then_inc(s_loaded[s], 16)
            sp.wait_ge(dvs.sem, dvs.before(("H", HGRN_HEADS)))
            gain_bias(1)
            ffn_loads(ffn_phases["F"], w2i, w2o)
            sp.wait_ge(s_xnew, TT + TL)
            gain_bias(2)
            for i in range(TL):
                sp.wait_ge(s_xnew, TT + TL + i + 1)
                sp.dma_start(out[i * P:(i + 1) * P, :], xtok[:, TC + i, :]).then_inc(s_out, 16)
            sp.wait_ge(s_out, 16 * TL)

        @block.gpsimd
        def _(pool):
            for i in range(2):
                nc.gpsimd.memset(attT[i][:, :, :], 0.0).then_inc(s_zero, 1)
            nc.gpsimd.memset(eps_ln[:, :], 1e-5).then_inc(s_zero, 1)
            nc.gpsimd.memset(eps_rms[:, :], 1e-6).then_inc(s_zero, 1)
            def ada(b):
                if not isinstance(b, int):
                    pool.wait_ge(s_ada_done, b)
                elif b >= 4:
                    pool.wait_ge(s_ada_done, b if b >= ADA_FIRST else b - 3)
                first = isinstance(b, int) and b < ADA_FIRST
                pool.dma_start(ada_slot(b if first else None)[:, :, :], wad[:, :, bass.ds(b * 256, 256)]
                               ).then_inc(s_ada_first[b % 4] if first else s_ada_loaded, 16)

            for b in range(ADA_FIRST):
                ada(b)
            for name in "AB":
                for n, _, p_in, p_out, _, _ in ffn_phases[name]:
                    for start, count in ((p_in, n // 2), (p_out, 4)):
                        if start in ada_plan:
                            off, extra = ada_plan[start]
                            with pool.Fori(start + off, start + off + count) as b:
                                ada(b)
                            if extra is not None:
                                ada(extra)
            pool.wait_ge(s_xn, 2 * TT)
            nc.gpsimd.memset(ctx_part[0:32, TOK:TOK + 512], 0.0).then_inc(s_a2z, 1)
            pool.wait_ge(s_a2z, 1)
            pool.dma_start(a2[0][0:16, :], t["gla_a2_fwd"]).then_inc(s_a2, 16)
            pool.dma_start(a2[1][16:32, :], t["gla_a2_bwd"]).then_inc(s_a2, 16)

        @block.scalar
        def _(act):
            def split_hi(s, p):
                act.wait_ge(s_loaded[s], p * 32 + 32)
                act.wait_ge(s_lo[s], p + SEED)
                act.wait_ge(s_done[s], p)
                nc.scalar.activation(w_hi[s][:, :], w_raw[s][:, :], ACT.Copy).then_inc(s_hi[s], 1)

            n_stat = [0]

            def std_of():
                n_stat[0] += 1
                act.wait_ge(s_stat, n_stat[0])
                nc.scalar.activation(std[:, :], mv[:, 1:2], ACT.Sqrt, bias=eps_ln[:, :]).then_inc(s_std, 1)

            def modulate(q):
                tt, s = pre_jobs[q]
                v = 1 if tt < TC else 0
                act.wait_ge(s_scale, (1, 3, 5)[s])
                act.wait_ge(s_turned, q + 1)
                act.wait_ge(s_h, q)
                act.wait_ge(s_hhi, q)
                for k in range(KT):
                    ins = nc.scalar.activation(hfull[:, k, :], turn[:, k * P:(k + 1) * P], ACT.Identity,
                                               bias=mods[:, (3 * s + 1) * KT + k, v:v + 1],
                                               scale=scale1[:, k, v:v + 1])
                ins.then_inc(s_mod, 1)
                act.wait_ge(s_mod, q + 1)
                nc.scalar.activation(h_hi[:, :, tt * P:(tt + 1) * P], hfull, ACT.Copy).then_inc(s_hhi, 1)

            def norms(posts, pres):
                for i in range(max(len(posts), len(pres))):
                    if posts:
                        std_of()
                    if posts and pres and i:
                        modulate(pres[i - 1])
                    if pres:
                        std_of()
                    if not posts and i:
                        modulate(pres[i - 1])
                if pres:
                    modulate(pres[-1])

            def ffn(phases, bufs, n, gate_count, gated, segs):
                hid_hi, _, yT, glu = bufs
                sg, hf = glu[:, 0:2, :], glu[:, 2:4, :]
                for j, (tiles, _, p_in, p_out, i0, _) in enumerate(phases):
                    with act.Fori(0, tiles // 2) as i:
                        p = i + p_in
                        act.wait_ge(s_done[0], p + 1)
                        split_hi(0, p + 1)
                        act.wait_ge(s_hf, i * 2 + 2 * i0 + SEED)
                        for u in range(2):
                            nc.scalar.activation(sg[:, u, :], psA[:, u, 0:n], ACT.Silu).then_inc(s_silu, 1)
                        act.wait_ge(s_done[1], p + 1)
                        split_hi(1, p + 1)
                        for u in range(2):
                            act.wait_ge(s_hf, i * 2 + (2 * i0 + u + 1) + SEED)
                            nc.scalar.activation(hid_hi[:, bass.ds(i * 2 + u, 1), :], hf[:, u:u + 1, :],
                                                 ACT.Copy).then_inc(s_hidhi, 1)

                    def out_pair(p, u, d):
                        act.wait_ge(s_done[0], p + 1)
                        split_hi(0, p + 1)
                        act.wait_ge(s_done[1], p + 1)
                        if j == 0:
                            for v in range(2):
                                nc.scalar.activation(yT[:, bass.ds(d + v, 1), :], psA[:, 2 * u + v:2 * u + v + 1, 0:n],
                                                     ACT.Copy).then_inc(s_y0, 1)

                    last = p_out + 3 == last_pair
                    if not last:
                        with act.Fori(0, 2) as hh:
                            for u in range(2):
                                p = hh * 2 + (p_out + u)
                                out_pair(p, u, hh * 4 + 2 * u)
                                split_hi(1, p + 1)
                    else:
                        for o in range(3):
                            out_pair(p_out + o, o % 2, 2 * o)
                            split_hi(1, p_out + o + 1)
                act.wait_ge(s_scale, gate_count)
                act.wait_ge(s_y1, y1_after[phases[0][2]] + SEED)
                for k in range(KT):
                    for v, a, b in segs:
                        ins = nc.scalar.activation(yT[:, k, a:b], yT[:, k, a:b], ACT.Copy,
                                                   scale=gate_w[:, k, v:v + 1])
                ins.then_inc(s_ygate, 1)

            for ring in (s_silu, s_y0):
                act.sem_inc(ring, SEED)
            act.wait_ge(s_cols, 1)
            nc.scalar.activation(small[:, 0:16], cols[:, R_C:R_C + 16], ACT.Silu).then_inc(s_silu_c, 1)
            act.wait_ge(s_own, 2)
            nc.scalar.activation(small[:, 16:32], small[:, 16:32], ACT.Exp).then_inc(s_lbe, 1)
            act.wait_ge(s_zero, 4)
            for s in range(2):
                split_hi(s, 0)
            norms([], range(TT))
            for g, (t0, nt) in enumerate(FFN1_GROUPS):
                segs = [(1, 0, TC * P), (0, TC * P, n1)] if g == 0 else [(0, 0, n1)]
                ffn(ffn_phases["AB"[g]], ffn1, n1, 2, g + 1, segs)
                norms(range(t0, t0 + nt), range(TT + t0, TT + t0 + nt))

            def mixer(g):
                kind, _ = g
                acs.start(g)
                p = mix_group_pair(g)
                prev = lambda: (act.wait_ge(dvs.sem, dvs.before(g)), act.wait_ge(pes.sem, pes.before(g)))

                def wait_self(name):
                    act.wait_ge(acs.sem, acs.at(g, name))

                def wait_dve(name):
                    act.wait_ge(dvs.sem, dvs.at(g, name))

                def wait_pe(name):
                    act.wait_ge(pes.sem, pes.at(g, name))

                def gating(d, s):
                    lat = slice(TC * P, TOK)
                    edge = CHUNK - 1 if d == 0 else 0
                    wait_dve(f"b{d}")
                    acs.done(nc.scalar.activation(qdec[d][:, :], T[4][:, lat], ACT.Exp, scale=s), f"eb{d}")
                    acs.done(nc.scalar.activation(T[0][:, lat], T[4][:, lat], ACT.Exp, scale=-s), f"einv{d}")
                    acs.done(nc.scalar.activation(
                        dec[d][:, :], T[4].rearrange("p (n c) -> p n c", c=CHUNK)[:, :, edge], ACT.Exp, scale=s),
                        f"dec{d}")
                    wait_dve(f"diff{d}")
                    acs.done(nc.scalar.activation(T[3], T[3], ACT.Exp, scale=s), f"tail{d}")

                prev()
                if kind == "G":
                    pr = g[1]
                    act.wait_ge(s_done[0], p + 1)
                    split_hi(0, p + 1)
                    acs.done(nc.scalar.activation(T[1][:, 0:2 * n1].rearrange("p (a b) -> p a b", b=n1),
                                                  psA[:, 0:2, 0:n1], ACT.Copy), "k")
                    act.wait_ge(s_done[1], p + 1)
                    acs.done(nc.scalar.activation(qf[:, :], psA[:, 2, :], ACT.Copy, scale=64.0 ** -0.5), "q")
                    if pr == 0:
                        nc.scalar.activation(lr.rearrange("p (a b) -> p a b", b=n1), psX[0:32, 0:2, 0:n1],
                                             ACT.Copy).then_inc(s_lr, 1)
                    split_hi(1, p + 1)
                    for d in range(2):
                        wait_pe(f"z{d}")
                        dst = T[0] if d == 0 else tail[1][:, :]
                        b0 = R_GBIAS + 2 * d + pr
                        acs.done(nc.scalar.activation(dst.rearrange("p (a b) -> p a b", b=n1),
                                                      psX[:, 2 * d:2 * d + 2, 0:n1], ACT.Identity,
                                                      bias=cols[:, b0:b0 + 1]), f"z{d}")
                    for d in range(2):
                        wait_self(f"z{d}")
                        z = T[0] if d == 0 else tail[1][:, :]
                        if d == 1:
                            wait_self("tail0")
                            wait_dve("tail0")
                        acs.done(nc.scalar.activation(T[2], z, ACT.Abs), f"abs{d}")
                        wait_self(f"abs{d}")
                        acs.done(nc.scalar.activation(T[2], T[2], ACT.Exp, scale=-1.0), f"ex{d}")
                        wait_self(f"ex{d}")
                        acs.done(nc.scalar.activation(T[2], T[2], ACT.Ln, bias=1.0), f"ln{d}")
                        gating(d, 1.0 / 16.0)
                else:
                    act.wait_ge(s_done[0], p + 1)
                    split_hi(0, p + 1)
                    acs.done(nc.scalar.activation(T[0].rearrange("p (a b) -> p a b", b=n1),
                                                  psA[:, 0:2, 0:n1], ACT.Sigmoid), "sig0")
                    act.wait_ge(s_done[1], p + 1)
                    split_hi(1, p + 1)
                    acs.done(nc.scalar.activation(tail[1][:, :].rearrange("p (a b) -> p a b", b=n1),
                                                  psA[:, 2:4, 0:n1], ACT.Sigmoid), "sig1")
                    for d in range(2):
                        wait_dve(f"f{d}")
                        acs.done(nc.scalar.activation(T[3], T[0], ACT.Ln), f"ln{d}")
                        gating(d, 1.0)
                for i, _, _ in heads_of(kind):
                    act.wait_ge(s_done[0], p + 2)
                    src = psX[:, 0:2, 0:n1] if kind == "H" else psA[:, 2 * i:2 * i + 2, 0:n1]
                    if i == 1:
                        wait_pe("vT0")
                    acs.done(nc.scalar.activation(vf.rearrange("p (a b) -> p a b", b=n1), src, ACT.Copy), f"vf{i}")
                    wait_pe(f"vT{i}")
                    acs.done(nc.scalar.activation(vtok[i][:, 0:4, :], psX[:, 0, :].rearrange("p (a b) -> p a b", b=P),
                                                  ACT.Copy), f"vt{i}a")
                    acs.done(nc.scalar.activation(vtok[i][:, 4:6, :],
                                                  psX[:, 1, 0:2 * P].rearrange("p (a b) -> p a b", b=P),
                                                  ACT.Copy), f"vt{i}b")
                if kind == "H":
                    act.wait_ge(s_done[1], p + 2)
                    acs.done(nc.scalar.activation(qf[:, :], psX[:, 2, :], ACT.Sigmoid), "sigq")
                    acs.done(nc.scalar.activation(gates[0][:, :], psX[:, 3, :], ACT.Sigmoid), "sigg0")
                else:
                    for i in range(2):
                        act.wait_ge(s_done[1], p + 2)
                        acs.done(nc.scalar.activation(gates[i][:, :], psX[:, 2 + i, :], ACT.Sigmoid), f"sigg{i}")
                for s in range(2):
                    split_hi(s, p + 2)
                for i, _, _ in heads_of(kind):
                    wait_pe(f"o{TL - 1}{i}")
                    if i == 1:
                        wait_pe("ms0")
                    acs.done(nc.scalar.activation(T[0][:, 0:SEQ], psX[:, 2 + i, :], ACT.Square), f"sq{i}")
                    wait_pe(f"ms{i}")
                    if i == 1:
                        wait_dve("on0")
                    acs.done(nc.scalar.activation(T[2][:, 0:SEQ], psX[:, i, :], ACT.Ln, bias=eps_rms[:, :],
                                                  scale=1.0 / P), f"lnms{i}")
                    wait_self(f"lnms{i}")
                    acs.done(nc.scalar.activation(T[3][:, 0:SEQ], T[2][:, 0:SEQ], ACT.Exp, scale=-0.5), f"rinv{i}")
                acs.end()

            for pr in range(GLA_PAIRS):
                mixer(("G", pr))
            with act.Fori(0, HGRN_HEADS) as h:
                mixer(("H", h))

            act.wait_ge(dvs.sem, dvs.before(("H", HGRN_HEADS)))
            for k in range(KT):
                nc.scalar.activation(h_hi[:, k, TC * P:TOK], mT[:, k, :], ACT.Copy).then_inc(s_mhi, 1)
            act.wait_ge(s_m, KT)
            act.wait_ge(s_scale, 4)
            for i in range(2):
                p = mix_out_pair + i
                for s in range(2):
                    act.wait_ge(s_done[s], p + 1)
                    split_hi(s, p + 1)
                    for u in range(2):
                        d = 4 * i + 2 * s + u
                        nc.scalar.activation(mT[:, d, :], psA[:, 2 * s + u, :], ACT.Copy,
                                             scale=gate_w[:, d, 0:1]).then_inc(s_mo, 1)
            norms(range(TT, TT + TL), range(2 * TT, 2 * TT + TL))
            ffn(ffn_phases["F"], ffn2, n2, 6, 3, [(0, 0, n2)])
            norms(range(TT + TL, TT + 2 * TL), [])

        @block.vector
        def _(dve):
            own = [0]

            def link(ins):
                own[0] += 1
                ins.then_inc(s_own, 1)
                dve.wait_ge(s_own, own[0])

            def split_lo(s, p):
                dve.wait_ge(s_hi[s], p + 1)
                nc.vector.tensor_tensor(w_lo[s][:, :], w_raw[s][:, :], w_hi[s][:, :].bitcast(F32),
                                        ALU.subtract).then_inc(s_lo[s], 1)

            def ada_take(b):
                dve.wait_ge(s_ada_done, b + 1)
                nc.vector.tensor_copy(ada_row[:, :], ada_row_ps).then_inc(s_ada_row, 1)

            def ada_out(b):
                dve.wait_ge(s_ada_turned, b + 1)
                bias = cols[:, bass.ds(b * 2, 2)].unsqueeze(2).to_broadcast([P, 2, 2])
                nc.vector.tensor_tensor(mods[:, bass.ds(b * 2, 2), :], ada_ps, bias, ALU.add).then_inc(s_ada_out, 1)

            n_stat = [0]

            def statistics(src):
                for i in range(2):
                    ins = nc.vector.bn_stats(stats[:, 6 * i:6 * i + 6], src[:, i * 512:(i + 1) * 512])
                link(ins)
                n_stat[0] += 1
                nc.vector.bn_aggr(mv[:, :], stats[:, :]).then_inc(s_stat, 1)
                dve.wait_ge(s_stat, n_stat[0])

            def reciprocal_std():
                dve.wait_ge(s_std, n_stat[0])
                link(nc.vector.reciprocal(rstd[:, :], std[:, :]))

            def pre(q):
                tt, s = pre_jobs[q]
                if q > 1:
                    dve.wait_ge(s_turned, q - 1)
                statistics(xtok[:, tt, :])
                reciprocal_std()
                nc.vector.tensor_scalar(xn_of(q), xtok[:, tt, :], mv[:, 0:1], rstd[:, 0:1],
                                        ALU.subtract, ALU.mult).then_inc(s_xn, 1)

            def low_part(q):
                tt, s = pre_jobs[q]
                dve.wait_ge(s_hhi, q + 1)
                nc.vector.tensor_tensor(h_lo[:, :, tt * P:(tt + 1) * P], hfull,
                                        h_hi[:, :, tt * P:(tt + 1) * P].bitcast(F32), ALU.subtract).then_inc(s_h, 1)

            def post(q):
                tt, s = post_jobs[q]
                x = xtok[:, tt, :]
                dve.wait_ge(s_yturned, q + 1)
                ins = nc.vector.scalar_tensor_tensor(out=x, in0=x, scalar=ALPHA, in1=turn_y, op0=ALU.mult, op1=ALU.add)
                ins.then_inc(s_r, 1)
                dve.wait_ge(s_r, q + 1)
                statistics(x)
                dve.wait_ge(s_gb, 32 * (s + 1))
                link(nc.vector.scalar_tensor_tensor(out=x, in0=x, scalar=mv[:, 0:1], in1=gain_b,
                                                    op0=ALU.subtract, op1=ALU.mult))
                reciprocal_std()
                nc.vector.scalar_tensor_tensor(out=x, in0=x, scalar=rstd[:, 0:1], in1=bias_b,
                                               op0=ALU.mult, op1=ALU.add).then_inc(s_xnew, 1)
                dve.wait_ge(s_xnew, q + 1)

            def norms(posts, pres, pre_done=0):
                for i in range(max(len(posts), len(pres))):
                    if posts:
                        post(posts[i])
                    if pres and i >= pre_done:
                        pre(pres[i])
                    if pres and i:
                        low_part(pres[i - 1])
                if pres:
                    low_part(pres[-1])

            def scale_of(s):
                dve.wait_ge(s_ada_out, min(12 * s + 8, ADA_BLOCKS))
                dve.wait_ge(s_mod, (0, TT, 2 * TT)[s])
                nc.vector.tensor_scalar(scale1[:, :, :], mods[:, 24 * s:24 * s + 8, :], 1.0, None,
                                        ALU.add).then_inc(s_scale, 1)

            def gate_of(s):
                dve.wait_ge(s_ada_out, 12 * s + 12)
                nc.vector.tensor_scalar(gate_w[:, :, :], mods[:, 24 * s + 16:24 * s + 24, :],
                                        1.0 if s == 1 else 0.5, None, ALU.mult).then_inc(s_scale, 1)

            def ffn(phases, bufs, n):
                hid_hi, hid_lo, yT, glu = bufs
                sg, hf = glu[:, 0:2, :], glu[:, 2:4, :]
                for j, (tiles, _, p_in, p_out, i0, _) in enumerate(phases):
                    with dve.Fori(0, tiles // 2) as i:
                        p = i + p_in
                        split_lo(0, p + 1)
                        if p_in in ada_plan:
                            ada_take(p + ada_plan[p_in][0])
                        dve.wait_ge(s_done[1], p + 1)
                        dve.wait_ge(s_hid, i * 2 + 2 * i0 + SEED)
                        for u in range(2):
                            dve.wait_ge(s_silu, i * 2 + (2 * i0 + u + 1) + SEED)
                            nc.vector.tensor_tensor(hf[:, u, :], psA[:, 2 + u, 0:n], sg[:, u, :],
                                                    ALU.mult).then_inc(s_hf, 1)
                        split_lo(1, p + 1)
                        for u in range(2):
                            dve.wait_ge(s_hidhi, i * 2 + (2 * i0 + u + 1))
                            nc.vector.tensor_tensor(hid_lo[:, bass.ds(i * 2 + u, 1), :], hf[:, u:u + 1, :],
                                                    hid_hi[:, bass.ds(i * 2 + u, 1), :].bitcast(F32),
                                                    ALU.subtract).then_inc(s_hid, 1)
                        if p_in in ada_plan:
                            ada_out(p + ada_plan[p_in][0])
                    if p_in in ada_plan and ada_plan[p_in][1] is not None:
                        ada_take(ada_plan[p_in][1])
                        ada_out(ada_plan[p_in][1])

                    def out_pair(p, u, d):
                        split_lo(0, p + 1)
                        if p_out in ada_plan:
                            ada_take(p + ada_plan[p_out][0])
                        dve.wait_ge(s_done[1], p + 1)
                        if j:
                            for v in range(2):
                                y = yT[:, bass.ds(d + v, 1), :]
                                nc.vector.tensor_tensor(y, psA[:, 2 * u + v:2 * u + v + 1, 0:n], y,
                                                        ALU.add).then_inc(s_y1, 1)

                    if j:
                        dve.wait_ge(s_y0, y0_after[p_out] + SEED)
                        dve.wait_ge(s_y1, y1_before[p_out] + SEED)
                    if p_out + 3 == last_pair:
                        for o in range(3):
                            out_pair(p_out + o, o % 2, 2 * o)
                            split_lo(1, p_out + o + 1)
                        dve.wait_ge(s_done[1], p_out + 4)
                        for v in range(2):
                            y = yT[:, 6 + v:7 + v, :]
                            nc.vector.tensor_tensor(y, psA[:, 2 + v:3 + v, 0:n], y, ALU.add).then_inc(s_y1, 1)
                    else:
                        with dve.Fori(0, 2) as hh:
                            for u in range(2):
                                p = hh * 2 + (p_out + u)
                                out_pair(p, u, hh * 4 + 2 * u)
                                split_lo(1, p + 1)
                                if p_out in ada_plan:
                                    ada_out(p + ada_plan[p_out][0])
                    if p_out in ada_plan and ada_plan[p_out][1] is not None:
                        ada_take(ada_plan[p_out][1])
                        ada_out(ada_plan[p_out][1])

            for ring in (s_lo[0], s_lo[1], s_hf, s_hid, s_y1):
                dve.sem_inc(ring, SEED)
            dve.wait_ge(s_cols_ps, 1)
            nc.vector.tensor_copy(cols[:, :], psX[:, 3, 0:N_ROWS]).then_inc(s_cols, 1)
            dve.wait_ge(s_cols, 1)
            lg = cols[:, R_LB:R_LB + 16].rearrange("p (d l h) -> p d l h", d=2, l=2)
            ex = small[:, 16:32].rearrange("p (d l h) -> p d l h", d=2, l=2)
            link(nc.vector.tensor_tensor(lb[:, :, :], lg[:, :, 0, :], lg[:, :, 1, :], ALU.max))
            for l in range(2):
                ins = nc.vector.tensor_tensor(ex[:, :, l, :], lg[:, :, l, :], lb[:, :, :], ALU.subtract)
            link(ins)
            dve.wait_ge(s_lbe, 1)
            link(nc.vector.tensor_tensor(lb1[:, :, :], ex[:, :, 0, :], ex[:, :, 1, :], ALU.add))
            link(nc.vector.reciprocal(lb1[:, :, :], lb1[:, :, :]))
            link(nc.vector.tensor_tensor(lb[:, :, :], ex[:, :, 0, :], lb1[:, :, :], ALU.mult))
            link(nc.vector.tensor_scalar(lb1[:, :, :], lb[:, :, :], -1.0, 1.0, ALU.mult, ALU.add))
            dve.wait_ge(s_x, 16 * (TT + 2 * TL + 1))
            for i in range(TL):
                x = xtok[:, TC + i, :]
                nc.vector.tensor_tensor(x[:, 0:512], x[:, 0:512], prow[i], ALU.add)
                ins = nc.vector.tensor_tensor(x[:, 512:D], x[:, 512:D], pcol, ALU.add)
            link(ins)
            for b in range(ADA_FIRST):
                ada_take(b)
                ada_out(b)
                if b in (4, 5):
                    pre(b - 4)
            scale_of(0)
            for s in range(2):
                split_lo(s, 0)
            norms([], range(TT), 2)
            for g, (t0, nt) in enumerate(FFN1_GROUPS):
                ffn(ffn_phases["AB"[g]], ffn1, n1)
                if g == 0:
                    gate_of(0)
                    scale_of(1)
                norms(range(t0, t0 + nt), range(TT + t0, TT + t0 + nt))

            def mixer(g):
                kind, n = g
                dvs.start(g)
                p = mix_group_pair(g)

                def wait_self(name):
                    dve.wait_ge(dvs.sem, dvs.at(g, name))

                def wait_act(name):
                    dve.wait_ge(acs.sem, acs.at(g, name))

                def wait_pe(name):
                    dve.wait_ge(pes.sem, pes.at(g, name))

                dve.wait_ge(dvs.sem, dvs.before(g))
                dve.wait_ge(pes.sem, pes.before(g))
                dve.wait_ge(acs.sem, acs.before(g))
                if kind == "H":
                    nc.vector.tensor_copy(lbh[:, 0, :], lb[:, :, bass.ds(n, 1)].rearrange("p a b -> p (a b)"))
                    dvs.done(nc.vector.tensor_copy(lbh[:, 1, :], lb1[:, :, bass.ds(n, 1)].rearrange("p a b -> p (a b)")),
                             "lb")
                    wait_self("lb")
                split_lo(0, p + 1)
                split_lo(1, p + 1)
                for d in range(2):
                    lat = slice(TC * P, TOK)
                    edge = CHUNK - 1 if d == 0 else 0
                    if kind == "H":
                        wait_act(f"sig{d}")
                        if d == 1:
                            wait_act("tail0")
                            wait_self("tail0")
                        src = T[0] if d == 0 else tail[1][:, :]
                        dvs.done(nc.vector.tensor_scalar(T[0], src, lbh[:, 1, d:d + 1], lbh[:, 0, d:d + 1],
                                                         ALU.mult, ALU.add), f"f{d}")
                        wait_self(f"f{d}")
                        dvs.done(nc.vector.tensor_scalar(T[1], T[0], -1.0, 1.0, ALU.mult, ALU.add), f"k{d}")
                        wait_act(f"ln{d}")
                    else:
                        wait_act(f"z{d}")
                        if d == 1:
                            wait_act("tail0")
                            wait_self("tail0")
                        src = T[0] if d == 0 else tail[1][:, :]
                        dvs.done(nc.vector.tensor_scalar(T[3], src, 0.0, None, ALU.min), f"zm{d}")
                        wait_self(f"zm{d}")
                        wait_act(f"ln{d}")
                        dvs.done(nc.vector.tensor_tensor(T[3], T[3], T[2], ALU.subtract), f"g{d}")
                        wait_self(f"g{d}")
                    lf, b = (T[3], T[4]) if d == 0 else (T[3][:, ::-1], T[4][:, ::-1])
                    dvs.done(nc.vector.tensor_tensor_scan(b, smask[:, :], lf, 0.0, ALU.mult, ALU.add), f"b{d}")
                    wait_self(f"b{d}")
                    b3 = T[4].rearrange("p (n c) -> p n c", c=CHUNK)
                    dvs.done(nc.vector.tensor_tensor(
                        T[3].rearrange("p (n c) -> p n c", c=CHUNK),
                        b3[:, :, edge:edge + 1].to_broadcast([P, NCH, CHUNK]), b3, ALU.subtract), f"diff{d}")
                    wait_act(f"einv{d}")
                    dvs.done(nc.vector.tensor_tensor(kinv[d][:, :], T[1][:, lat], T[0][:, lat], ALU.mult), f"kinv{d}")
                    wait_act(f"tail{d}")
                    dvs.done(nc.vector.tensor_tensor(tail[d][:, :], T[1], T[3], ALU.mult), f"tail{d}")
                def mask_tail(s):
                    for d in range(2):
                        m = 2 * s + d
                        wait_pe(f"T{m}")
                        if m >= 2:
                            wait_pe(f"U{m - 2}")
                        dvs.done(nc.vector.tensor_tensor(
                            kt4[d][:, :, :], tail_ps(m).unsqueeze(1).to_broadcast([P, CPT, P]),
                            cmask[:, :].unsqueeze(2).to_broadcast([P, CPT, P]), ALU.mult), f"kt{m}")

                mask_tail(0)
                for s in range(TT):
                    if s + 1 < TT:
                        mask_tail(s + 1)
                    for c in range(CPT):
                        j = s * CPT + c
                        for d in range(2):
                            if j >= NCH - 1:
                                continue
                            if c == 0:
                                wait_pe(f"U{2 * s + d}")
                            lc = c if d == 0 else CPT - 1 - c
                            ch = scan_tiles(d)[s] * CPT + lc
                            u = psA[:, 2 * (s % 2) + d, lc * P:(lc + 1) * P]
                            new = CC - 1 - j if j < CC else j - CC + 1
                            old = CC - j if j < CC else j - CC
                            if j == 0:
                                ins = nc.vector.tensor_copy(St[d][:, new, :], u)
                            else:
                                wait_self(f"S{d}_{j - 1}")
                                ins = nc.vector.scalar_tensor_tensor(
                                    out=St[d][:, new, :], in0=St[d][:, old, :], scalar=dec[d][:, ch:ch + 1],
                                    in1=u, op0=ALU.mult, op1=ALU.add)
                            dvs.done(ins, f"S{d}_{j}")
                    if s == 0 and kind == "H":
                        wait_act("sigg0")
                        dvs.done(nc.vector.scalar_tensor_tensor(out=qf[:, :], in0=qf[:, :], scalar=128.0 ** -0.5,
                                                                in1=psX[:, 2, :], op0=ALU.mult, op1=ALU.mult), "q")
                        dvs.done(nc.vector.tensor_tensor(gates[0][:, :], gates[0][:, :], psX[:, 3, :], ALU.mult),
                                 "gate0")
                        wait_self("q")
                    elif s == 0:
                        for i in range(2):
                            wait_act(f"sigg{i}")
                            dvs.done(nc.vector.tensor_tensor(gates[i][:, :], gates[i][:, :], psX[:, 2 + i, :],
                                                             ALU.mult), f"gate{i}")
                    elif s <= 2:
                        d = s - 1
                        dvs.done(nc.vector.tensor_tensor(qdec[d][:, :], qf[:, :], qdec[d][:, :], ALU.mult), f"qdec{d}")
                    elif s == 3:
                        split_lo(0, p + 2)
                seq = [f"{tt}{i}" for tt in range(TL) for i, _, _ in heads_of(kind)]
                for at, job in enumerate(seq):
                    for d in range(2):
                        wait_pe(f"att{job}{d}")
                        if at >= 2:
                            wait_pe(f"o{seq[at - 2]}")
                            wait_self(f"am{seq[at - 2]}{d}")
                        dve.sem_inc(s_mask_turn, 1)
                        dvs.done(nc.vector.copy_predicated(attT[at % 2][:, d, :], amask[:, d, :],
                                                           psA[:, (0, 2)[at % 2] + d, 0:P]), f"am{job}{d}")
                split_lo(1, p + 2)
                for i, _, _ in heads_of(kind):
                    gcol = R_GAIN if kind == "G" else R_GAIN + 1
                    wait_act(f"sq{i}")
                    if i == 1:
                        wait_self("m0")
                    dvs.done(nc.vector.tensor_scalar(T[1][:, 0:SEQ], psX[:, 2 + i, :], cols[:, gcol:gcol + 1], None,
                                                     ALU.mult), f"og{i}")
                    wait_self(f"og{i}")
                    wait_act(f"rinv{i}")
                    dvs.done(nc.vector.tensor_tensor(T[1][:, 0:SEQ], T[1][:, 0:SEQ], T[3][:, 0:SEQ], ALU.mult),
                             f"on{i}")
                    wait_self(f"on{i}")
                    dst = mT[:, 2 * n + i:2 * n + i + 1, :] if kind == "G" else mT[:, bass.ds(n + 4, 1), :]
                    dvs.done(nc.vector.tensor_tensor(dst, T[1][:, 0:SEQ].unsqueeze(1), gates[i][:, :].unsqueeze(1),
                                                     ALU.mult), f"m{i}")
                dvs.end()

            for pr in range(GLA_PAIRS):
                mixer(("G", pr))
            with dve.Fori(0, HGRN_HEADS) as h:
                mixer(("H", h))
            for k in range(KT):
                dve.wait_ge(s_mhi, k + 1)
                nc.vector.tensor_tensor(h_lo[:, k, TC * P:TOK], mT[:, k, :],
                                        h_hi[:, k, TC * P:TOK].bitcast(F32), ALU.subtract).then_inc(s_m, 1)
            gate_of(1)
            scale_of(2)
            for i in range(2):
                for s in range(2):
                    split_lo(s, mix_out_pair + i + 1)
            norms(range(TT, TT + TL), range(2 * TT, 2 * TT + TL))
            ffn(ffn_phases["F"], ffn2, n2)
            gate_of(2)
            norms(range(TT + TL, TT + 2 * TL), [])

        @block.tensor
        def _(pe):
            def product(dst, w_h, w_l, x_h, x_l, start, stop):
                nc.tensor.matmul(dst, w_l, x_h, start=start, stop=False)
                nc.tensor.matmul(dst, w_h, x_l, start=False, stop=False)
                return nc.tensor.matmul(dst, w_h, x_h, start=False, stop=stop)

            def project(s, view, c, width, cells, ready=None):
                for dst, a, n in cells:
                    for k in range(KT):
                        if ready is not None:
                            pe.wait_ge(ready, k + 1)
                        ins = product(dst, view(w_hi[s])[:, k, c:c + width], view(w_lo[s])[:, k, c:c + width],
                                      h_hi[:, k, a:a + n], h_lo[:, k, a:a + n], k == 0, k == KT - 1)
                return ins

            def ada(b):
                first = isinstance(b, int) and b < ADA_FIRST
                w_a = ada_slot(b if first else None)
                if first:
                    pe.wait_ge(s_ada_first[b % 4], 16 * (b // 4 + 1))
                else:
                    pe.wait_ge(s_ada_loaded, b * 16 - 16 * (ADA_FIRST - 1))
                pe.wait_ge(s_ada_row, b)
                for k in range(KT):
                    ins = nc.tensor.matmul(ada_row_ps, small[:, k:16:KT], w_a[:, k, :], start=k == 0, stop=k == KT - 1)
                ins.then_inc(s_ada_done, 1)

            def ada_turn(b):
                pe.wait_ge(s_ada_row, b + 1)
                pe.wait_ge(s_ada_out, b)
                for j in range(2):
                    ins = nc.tensor.matmul(ada_ps[:, j, :], ada_row[:, j * P:(j + 1) * P], ident[0:2, 0:2],
                                           start=True, stop=True)
                ins.then_inc(s_ada_turned, 1)

            def pre(q):
                pe.wait_ge(s_xn, q + 1)
                pe.wait_ge(s_mod, q)
                for k in range(KT):
                    ins = nc.tensor.transpose(turn[:, k * P:(k + 1) * P], xn_of(q)[:, k * P:(k + 1) * P], ident[:, :])
                ins.then_inc(s_turned, 1)

            def post(q, yT, c0):
                pe.wait_ge(s_r, q)
                for k in range(KT):
                    ins = nc.tensor.transpose(turn_y[:, k * P:(k + 1) * P], yT[:, k, c0:c0 + P], ident[:, :])
                ins.then_inc(s_yturned, 1)

            def norms(posts, pres, yT=None):
                for i in range(len(posts) or len(pres)):
                    if posts and i == 0:
                        post(posts[0], yT, 0)
                    if i + 1 < len(posts):
                        post(posts[i + 1], yT, (i + 1) * P)
                    if pres:
                        pre(pres[i])

            def ffn(phases, bufs, n, c0):
                hid_hi, hid_lo, yT, _ = bufs
                view = lambda w: slot_view(w, KT, 256)
                for j, (tiles, _, p_in, p_out, i0, _) in enumerate(phases):
                    if j:
                        pe.wait_ge(s_y0, y0_after[p_in] + SEED)
                        pe.wait_ge(s_y1, y1_before[p_in] + SEED)
                    with pe.Fori(0, tiles // 2) as i:
                        p = i + p_in
                        for s, free in ((0, s_silu), (1, s_hf)):
                            pe.wait_ge(s_lo[s], p + 1 + SEED)
                            pe.wait_ge(free, i * 2 + 2 * i0 + SEED)
                            for u in range(2):
                                ins = project(s, view, u * P, P, [(psA[:, 2 * s + u, 0:n], c0, n)])
                            ins.then_inc(s_done[s], 1)
                            if s == 0 and p_in in ada_plan:
                                ada(p + ada_plan[p_in][0])
                        if p_in in ada_plan:
                            ada_turn(p + ada_plan[p_in][0])
                    if p_in in ada_plan and ada_plan[p_in][1] is not None:
                        ada(ada_plan[p_in][1])
                        ada_turn(ada_plan[p_in][1])

                    pe.wait_ge(s_silu, 2 * i0 + tiles + SEED)

                    def out_pair(p, u):
                        kk = tiles // 2
                        for s in range(2):
                            pe.wait_ge(s_lo[s], p + 1 + SEED)
                            pe.wait_ge(s_hid, 2 * i0 + (kk, tiles)[s] + SEED)
                            for v in range(2):
                                for k in range(kk):
                                    hk = s * kk + k
                                    c = slice(v * P, (v + 1) * P)
                                    ins = product(psA[:, 2 * u + v, 0:n], slot_view(w_hi[s], kk, 256)[:, k, c],
                                                  slot_view(w_lo[s], kk, 256)[:, k, c], hid_hi[:, hk, :],
                                                  hid_lo[:, hk, :], hk == 0, hk == tiles - 1)
                            ins.then_inc(s_done[s], 1)
                            if s == 0 and p_out in ada_plan:
                                ada(p + ada_plan[p_out][0])
                        if p_out in ada_plan:
                            ada_turn(p + ada_plan[p_out][0])

                    with pe.Fori(0, 2) as hh:
                        for u in range(2):
                            p = hh * 2 + (p_out + u)
                            if j == 0:
                                pe.wait_ge(s_y0, hh * 4 + y0_wait[p_out][u] + SEED)
                            else:
                                pe.wait_ge(s_y1, hh * 4 + y1_wait[p_out][u] + SEED)
                            out_pair(p, u)
                    if p_out in ada_plan and ada_plan[p_out][1] is not None:
                        ada(ada_plan[p_out][1])
                        ada_turn(ada_plan[p_out][1])

            pe.wait_ge(s_const, 16 * 13)
            nc.tensor.transpose(psX[:, 3, 0:N_ROWS], rows[0:N_ROWS, :], ident[0:N_ROWS, 0:N_ROWS]).then_inc(s_cols_ps, 1)
            pe.wait_ge(s_silu_c, 1)
            for b in range(ADA_FIRST):
                ada(b)
                ada_turn(b)
            norms([], range(TT))
            pe.wait_ge(s_h, TT)
            for g, (t0, nt) in enumerate(FFN1_GROUPS):
                ffn(ffn_phases["AB"[g]], ffn1, n1, t0 * P)
                pe.wait_ge(s_ygate, g + 1)
                pe.wait_ge(s_ada_out, ada_after[g])
                norms(range(t0, t0 + nt), range(TT + t0, TT + t0 + nt), ffn1[2])

            def mixer(g):
                kind, n = g
                pes.start(g)
                p = mix_group_pair(g)
                heads = heads_of(kind)

                def wait_act(name):
                    pe.wait_ge(acs.sem, acs.at(g, name))

                def wait_dve(name):
                    pe.wait_ge(dvs.sem, dvs.at(g, name))

                def all_tokens(bank):
                    return [(psA[:, bank, 0:n1], 0, n1), (psA[:, bank + 1, 0:n1], n1, n1)]

                def wait_before():
                    pe.wait_ge(acs.sem, acs.before(g))
                    pe.wait_ge(dvs.sem, dvs.before(g))

                one = lambda w: slot_view(w, KT, P)
                second = lambda w: slot_view(w, 2 * KT, P)[:, KT:2 * KT, :]
                wide = lambda w: slot_view(w, KT, 256)
                x_all = [(psX[:, 0, 0:n1], 0, n1), (psX[:, 1, 0:n1], n1, n1)]
                pe.wait_ge(s_lo[0], p + 1 + SEED)
                if kind == "H":
                    project(0, one, 0, P, all_tokens(0)).then_inc(s_done[0], 1)
                    pe.wait_ge(s_lo[1], p + 1 + SEED)
                    project(1, one, 0, P, all_tokens(2)).then_inc(s_done[1], 1)
                    wait_before()
                    pe.wait_ge(s_lo[0], p + 2 + SEED)
                    project(0, one, 0, P, x_all).then_inc(s_done[0], 1)
                    pe.wait_ge(s_lo[1], p + 2 + SEED)
                    project(1, one, 0, P, [(psX[:, 2, :], TC * P, SEQ)])
                    project(1, second, 0, P, [(psX[:, 3, :], TC * P, SEQ)]).then_inc(s_done[1], 1)
                else:
                    ins = project(0, one, 0, P, all_tokens(0))
                    if n == 0:
                        ins = project(0, second, 0, P, [(psA[:, 2, :], TC * P, SEQ)])
                    ins.then_inc(s_done[0], 1)
                    pe.wait_ge(s_lo[1], p + 1 + SEED)
                    if n == 0:
                        wait_before()
                        low = lambda w: slot_view(w, KT, 32)
                        ins = project(1, low, 0, 32, [(psX[0:32, i, 0:n1], i * n1, n1) for i in range(2)])
                    else:
                        ins = project(1, one, 0, P, [(psA[:, 2, :], TC * P, SEQ)])
                    ins.then_inc(s_done[1], 1)
                    wait_before()
                    pe.wait_ge(s_lr, 1)
                    pe.wait_ge(s_a2, 32)
                    for d in range(2):
                        for i in range(2):
                            ins = nc.tensor.matmul(psX[:, 2 * d + i, 0:n1], a2[d][:, n * P:(n + 1) * P],
                                                   lr[:, i * n1:(i + 1) * n1], start=True, stop=True)
                        pes.done(ins, f"z{d}")
                    wait_act("q")
                    pe.wait_ge(s_lo[0], p + 2 + SEED)
                    for i in range(2):
                        ins = project(0, wide, i * P, P, all_tokens(2 * i))
                    ins.then_inc(s_done[0], 1)
                    wait_act("z1")
                    pe.wait_ge(s_lo[1], p + 2 + SEED)
                    for i in range(2):
                        ins = project(1, wide, i * P, P, [(psX[:, 2 + i, :], TC * P, SEQ)])
                    ins.then_inc(s_done[1], 1)
                def turn_tail(m):
                    s, d = m // 2, m % 2
                    if s == 0:
                        wait_dve(f"tail{d}")
                    else:
                        wait_dve(f"kt{m - 2}")
                    tt = scan_tiles(d)[s]
                    pes.done(nc.tensor.transpose(tail_ps(m), tail[d][:, tt * P:(tt + 1) * P], ident[:, :]),
                             f"T{m}")

                for i, _, _ in heads:
                    wait_act(f"vf{i}")
                    if i == heads[-1][0]:
                        turn_tail(0)
                        turn_tail(1)
                    if i == 1:
                        wait_act("vt0b")
                    for tt in range(TT):
                        dst = psX[:, tt // 4, (tt % 4) * P:(tt % 4 + 1) * P]
                        ins = nc.tensor.transpose(dst, vf[:, tt * P:(tt + 1) * P], ident[:, :])
                    pes.done(ins, f"vT{i}")
                wait_act(f"vt{heads[-1][0]}b")

                for m in range(2 * TT):
                    if 1 <= m < 2 * TT - 1:
                        turn_tail(m + 1)
                    s, d = m // 2, m % 2
                    tt = scan_tiles(d)[s]
                    wait_dve(f"kt{m}")
                    if s >= 2:
                        wait_dve(f"S{d}_{(s - 1) * CPT - 1}")
                    for c in range(CPT):
                        for i, p0, pn in heads:
                            ins = nc.tensor.matmul(psA[p0:p0 + pn, 2 * (s % 2) + d, c * P:(c + 1) * P],
                                                   kt4[d][:, c, p0:p0 + pn], vtok[i][:, tt, :],
                                                   start=True, stop=True, skip_group_check=True)
                    pes.done(ins, f"U{m}")
                wait_dve("qdec1")
                seq = [(a, i) for a in range(TL) for i, _, _ in heads]

                def attention(at):
                    tt, i = seq[at]
                    _, p0, pn = heads[i]
                    cols_t = slice(tt * P, (tt + 1) * P)
                    for d in range(2):
                        if at >= 2:
                            wait_dve(f"am{seq[at - 2][0]}{seq[at - 2][1]}{d}")
                        pes.done(nc.tensor.matmul(psA[:, (0, 2)[at % 2] + d, 0:P], kinv[d][p0:p0 + pn, cols_t],
                                                  qdec[d][p0:p0 + pn, cols_t], start=True, stop=True), f"att{tt}{i}{d}")

                for d in range(2):
                    wait_dve(f"S{d}_{(TT - 1) * CPT - 1}")
                attention(0)
                for d in range(2):
                    wait_dve(f"S{d}_{NCH - 2}")
                for at, (tt, i) in enumerate(seq):
                    if at + 1 < len(seq):
                        attention(at + 1)
                    _, p0, pn = heads[i]
                    cols_t = slice(tt * P, (tt + 1) * P)
                    o = psX[:, 2 + i, :]
                    for d in range(2):
                        wait_dve(f"am{tt}{i}{d}")
                        nc.tensor.matmul(o[:, cols_t], vtok[i][:, TC + tt, :], attT[at % 2][:, d, :],
                                         start=d == 0, stop=False, skip_group_check=True)
                    for d in range(2):
                        for c in range(CPT):
                            ch = tt * CPT + c
                            m = ch if d == 0 else LC - 1 - ch
                            cc = slice(ch * CHUNK, (ch + 1) * CHUNK)
                            ins = nc.tensor.matmul(o[:, cc], St[d][p0:p0 + pn, m, :], qdec[d][p0:p0 + pn, cc],
                                                   start=False, stop=True, skip_group_check=True)
                    pes.done(ins, f"o{tt}{i}")
                for i, _, _ in heads:
                    wait_act(f"sq{i}")
                    pes.done(nc.tensor.matmul(psX[:, i, :], ones[:, :], T[0][:, 0:SEQ], start=True, stop=True),
                             f"ms{i}")
                pes.end()

            pe.wait_ge(s_h, 2 * TT)
            for pr in range(GLA_PAIRS):
                mixer(("G", pr))
            with pe.Fori(0, HGRN_HEADS) as h:
                mixer(("H", h))
            pe.wait_ge(acs.sem, acs.before(("H", HGRN_HEADS)))
            for i in range(2):
                for s in range(2):
                    pe.wait_ge(s_lo[s], mix_out_pair + i + 1 + SEED)
                    if i:
                        pe.wait_ge(s_mo, 2 * s + 2)
                    for u in range(2):
                        ins = project(s, lambda w: slot_view(w, KT, 256), u * P, P,
                                      [(psA[:, 2 * s + u, :], TC * P, SEQ)], s_m if i + s + u == 0 else None)
                    ins.then_inc(s_done[s], 1)
            pe.wait_ge(s_mo, KT)
            norms(range(TT, TT + TL), range(2 * TT, 2 * TT + TL), mT)
            pe.wait_ge(s_h, len(pre_jobs))
            ffn(ffn_phases["F"], ffn2, n2, TC * P)
            pe.wait_ge(s_ygate, 3)
            norms(range(TT + TL, TT + 2 * TL), [], ffn2[2])


def position_rows():
    import numpy as np

    quarter = D // 4
    omega = np.float32(1.0) / np.power(np.float32(10000.0), np.arange(quarter, dtype=np.float32) / np.float32(quarter))

    def emb(n):
        a = np.arange(n).astype(np.float32)[:, None] * omega.astype(np.float32)[None, :]
        return np.concatenate([np.sin(a), np.cos(a)], axis=-1).astype(np.float32)

    return emb(SEQ // 64), np.tile(emb(64), (2, 1))


def constants():
    import numpy as np

    j, i = np.meshgrid(np.arange(P), np.arange(P), indexing="ij")
    same = j // CHUNK == i // CHUNK
    prow, pcol = position_rows()
    starts = np.where(np.arange(TOK) % CHUNK == 0, 0.0, 1.0)
    return {
        "k_ident": np.eye(P, dtype=np.float32),
        "k_ones": np.ones((P, P), np.float32),
        "k_cmask": (j[:, 0:1] // CHUNK == np.arange(CPT)[None, :]).astype(np.float32),
        "k_smask": np.tile(starts[None, :], (P, 1)).astype(mybir.dt.np(mybir.dt.bfloat16)),
        "k_amask": np.stack([same & (j <= i), same & (j >= i)], axis=1).astype(np.int32),
        "k_prow": prow,
        "k_pcol": pcol,
    }


def kernel(**inputs):
    import numpy as np
    import concourse.bacc as bacc
    from concourse.bass_utils import run_bass_kernel_spmd as run

    shapes = {
        "x": (SEQ, D), "ctx": (CTX, D), "c": (8, P), "c_ctx": (8, P), "w_ada": (D, 9 * D), "b_ada": (72, P),
        "ln_gain": (3, D), "ln_bias": (3, D), "ffn1_w_in": (D, 2 * FF), "ffn1_w_out": (FF, D),
        "w_mix_in": (D, 4128), "gla_a2_fwd": (16, 256), "gla_a2_bwd": (16, 256), "gla_a_bias_fwd": (2, P),
        "gla_a_bias_bwd": (2, P), "hgrn_lb_logits": (16, P), "gla_norm_gain": (1, P), "hgrn_norm_gain": (1, P),
        "w_mix_out": (D, D), "ffn2_w_in": (D, 2 * FF), "ffn2_w_out": (FF, D),
    }
    arrays = {n: np.ascontiguousarray(inputs[n]).reshape(s) for n, s in shapes.items()}
    arrays.update(constants())
    nc = bacc.Bacc("TRN2", target_bir_lowering=False, num_devices=1)
    tensors = {n: nc.dram_tensor(n, a.shape, mybir.dt.from_np(a.dtype), kind="ExternalInput").ap()
               for n, a in arrays.items()}
    out = nc.dram_tensor("out", (SEQ, D), F32, kind="ExternalOutput").ap()
    build(nc, tensors, out)
    result = run(nc, [arrays], core_ids=[0])
    return result.results[0]["out"].reshape(1, SEQ, D)
```
